# Optimizing a Trainium2 kernel written in Bass

```python
import math, functools
import jax, jax.numpy as jnp
from jax import lax
import numpy as np

'''One inference step of a 2-layer chunk-causal hybrid streaming encoder, run for two request
groups with shared weights.

Layer l even : h += W_out[ concat( PoolMix(u), DSA(q,k,v,q_idx,k_idx,w_idx) ) ],  [u|q|k|v|q_idx|k_idx|w_idx] = RMSNorm(h) @ W_in
Layer l odd  : h += W_out[ concat( StickBreak(q,k,v), DiffAttn(q1,q2,k1,k2,v) ) ], one combined W_in
every layer  : h += HierMoE(RMSNorm(h))   (top-1 expert group, then top-2 experts in that group)
end          : y = RMSNorm(h)

Inputs (N_EVEN = (DEPTH+1)//2 even layers, N_ODD = DEPTH//2 odd layers):
  x_prompt     (BATCH, SEQ, D_MODEL)         first SEQ frames of new streams, positions 0..SEQ-1
  x_sample     (DEC_BATCH, DEC_SEQ, D_MODEL) next frames, positions PAST_LEN..PAST_LEN+DEC_SEQ-1
  cache_pool   (N_EVEN, DEC_BATCH, POOL_HIST, POOL_DIM)         last 15 pool-input rows
  cache_dsa_k  (N_EVEN, DEC_BATCH, PAST_LEN, DSA_KV_HEADS, HEAD_DIM)  rotated keys
  cache_dsa_v  (N_EVEN, DEC_BATCH, PAST_LEN, DSA_KV_HEADS, HEAD_DIM)
  cache_idx_k  (N_EVEN, DEC_BATCH, PAST_LEN, IDX_DIM)          rotated indexer keys
  cache_sb_k   (N_ODD, DEC_BATCH, PAST_LEN, SB_HEADS, HEAD_DIM)
  cache_sb_v   (N_ODD, DEC_BATCH, PAST_LEN, SB_HEADS, HEAD_DIM)
  cache_diff_k (N_ODD, DEC_BATCH, PAST_LEN, DIFF_HEADS, 2, HEAD_DIM) rotated keys of both maps
  cache_diff_v (N_ODD, DEC_BATCH, PAST_LEN, DIFF_HEADS, 2*HEAD_DIM)
  followed by all weights.

Returns the tuple
  (y_prompt (BATCH,SEQ,D), y_sample (DEC_BATCH,DEC_SEQ,D),
   pool_p (N_EVEN,BATCH,POOL_HIST,POOL_DIM), dsa_k_p (N_EVEN,BATCH,SEQ,2,64), dsa_v_p, idx_k_p (N_EVEN,BATCH,SEQ,64),
   sb_k_p (N_ODD,BATCH,SEQ,8,64), sb_v_p, diff_k_p (N_ODD,BATCH,SEQ,4,2,64), diff_v_p (N_ODD,BATCH,SEQ,4,128),
   pool_s (N_EVEN,DEC_BATCH,POOL_HIST,POOL_DIM), dsa_k_s (N_EVEN,DEC_BATCH,DEC_SEQ,2,64), dsa_v_s, idx_k_s,
   sb_k_s, sb_v_s, diff_k_s, diff_v_s)   (sample rows have DEC_SEQ rows; pool_s is the rolled 15-row buffer)
'''

D_MODEL = 1024
BATCH = 1
SEQ = 512
DEPTH = 2
DEC_BATCH = 1
DEC_SEQ = 32
PAST_LEN = 256

CHUNK = 64
Q_BLOCK = 128
HEAD_DIM = 64
ROPE_THETA = 10000.0
NORM_EPS = 1e-6
NEG_INF = -1e30
POOL_WINDOWS = (2, 4, 8, 16)
POOL_GROUPS = len(POOL_WINDOWS)
POOL_DIM = D_MODEL // 2
POOL_GROUP_DIM = POOL_DIM // POOL_GROUPS
POOL_HIST = max(POOL_WINDOWS) - 1
DSA_HEADS = (D_MODEL // 2) // HEAD_DIM
DSA_KV_HEADS = 2
DSA_TOPK = 256
IDX_HEADS = 4
IDX_DIM = 64
SB_HEADS = (D_MODEL // 2) // HEAD_DIM
DIFF_HEADS = (D_MODEL // 2) // (2 * HEAD_DIM)
MOE_GROUPS = 4
MOE_EXPERTS_PER_GROUP = 4
MOE_EXPERTS = MOE_GROUPS * MOE_EXPERTS_PER_GROUP
MOE_TOPK_INNER = 2
MOE_HIDDEN = D_MODEL // 2

N_EVEN = (DEPTH + 1) // 2
N_ODD = DEPTH // 2
EVEN_WIDTHS = (POOL_DIM, DSA_HEADS * HEAD_DIM, DSA_KV_HEADS * HEAD_DIM, DSA_KV_HEADS * HEAD_DIM,
               IDX_HEADS * IDX_DIM, IDX_DIM, IDX_HEADS)
EVEN_IN = sum(EVEN_WIDTHS)
EVEN_MIX = POOL_DIM + DSA_HEADS * HEAD_DIM
ODD_WIDTHS = (SB_HEADS * HEAD_DIM,) * 3 + (DIFF_HEADS * 2 * HEAD_DIM,) * 3
ODD_IN = sum(ODD_WIDTHS)
ODD_MIX = SB_HEADS * HEAD_DIM + DIFF_HEADS * 2 * HEAD_DIM

kernel_name = 'hybrid_stream_pool_dsa_stickbreak_diff_hmoe'

def _split_points(widths):
    return [int(v) for v in np.cumsum(widths)[:-1]]

def rmsnorm(x, g):
    xf = x.astype(jnp.float32)
    y = xf * lax.rsqrt(jnp.mean(xf * xf, axis=-1, keepdims=True) + NORM_EPS)
    return (y * g.astype(jnp.float32)).astype(x.dtype)

def rope(x, pos):
    half = x.shape[-1] // 2
    inv = ROPE_THETA ** (-jnp.arange(half, dtype=jnp.float32) / half)
    ang = pos.astype(jnp.float32)[:, None] * inv[None, :]
    shape = (1, pos.shape[0]) + (1,) * (x.ndim - 3) + (half,)
    cos, sin = jnp.cos(ang).reshape(shape), jnp.sin(ang).reshape(shape)
    xf = x.astype(jnp.float32)
    x1, x2 = xf[..., :half], xf[..., half:]
    return jnp.concatenate([x1 * cos - x2 * sin, x2 * cos + x1 * sin], axis=-1).astype(x.dtype)

def chunk_end(pos):
    return (pos // CHUNK + 1) * CHUNK

def sweep_queries(fn, q_args, q_pos):
    tq = q_pos.shape[0]
    if tq <= Q_BLOCK or tq % Q_BLOCK != 0:
        return fn(*q_args, q_pos)
    nb = tq // Q_BLOCK
    blocks = tuple(jnp.moveaxis(a.reshape((a.shape[0], nb, Q_BLOCK) + a.shape[2:]), 1, 0) for a in q_args)
    out = lax.map(lambda xs: fn(*xs), blocks + (q_pos.reshape(nb, Q_BLOCK),))
    out = jnp.moveaxis(out, 0, 1)
    return out.reshape((out.shape[0], tq) + out.shape[3:])

def pool_mix(u_ext, pos, w_pool, pool_scale):
    t = pos.shape[0]
    cs = jnp.cumsum(u_ext.astype(jnp.float32), axis=1)
    cs = jnp.pad(cs, ((0, 0), (1, 0), (0, 0)))
    u_new = u_ext[:, POOL_HIST:].astype(jnp.float32)
    outs = []
    for g, win in enumerate(POOL_WINDOWS):
        c0, c1 = g * POOL_GROUP_DIM, (g + 1) * POOL_GROUP_DIM
        hi = cs[:, POOL_HIST + 1:, c0:c1]
        lo = cs[:, POOL_HIST + 1 - win:POOL_HIST + 1 - win + t, c0:c1]
        cnt = jnp.minimum(pos + 1, win).astype(jnp.float32)[None, :, None]
        d = ((hi - lo) / cnt - u_new[..., c0:c1]).astype(u_ext.dtype)
        outs.append(d @ w_pool[g])
    return jnp.concatenate(outs, axis=-1) * pool_scale

def dsa_attend(q, qi, wi, q_pos, *, k, v, ki, k_pos, n_sel):
    b, tq, h, dh = q.shape
    g = k.shape[2]
    s_idx = jax.nn.relu(jnp.einsum('bthd,bsd->bths', qi, ki).astype(jnp.float32))
    s_idx = jnp.einsum('bths,bth->bts', s_idx, wi.astype(jnp.float32))
    lim = chunk_end(q_pos)
    adm = k_pos[None, :] < lim[:, None]
    s_idx = jnp.where(adm[None], s_idx, NEG_INF)
    _, sel = lax.top_k(s_idx, n_sel)
    valid = k_pos[sel] < lim[None, :, None]
    ks = jax.vmap(lambda kb, ib: kb[ib])(k, sel)
    vs = jax.vmap(lambda vb, ib: vb[ib])(v, sel)
    qg = q.reshape(b, tq, g, h // g, dh)
    sc = jnp.einsum('btgrd,btkgd->btgrk', qg, ks).astype(jnp.float32) * dh ** -0.5
    sc = jnp.where(valid[:, :, None, None, :], sc, NEG_INF)
    p = jax.nn.softmax(sc, axis=-1)
    o = jnp.einsum('btgrk,btkgd->btgrd', p.astype(vs.dtype), vs)
    return o.reshape(b, tq, h * dh)

def sb_attend(q, q_pos, *, k, v, k_pos):
    b, tq, h, dh = q.shape
    z = jnp.einsum('bthd,bshd->bhts', q, k).astype(jnp.float32) * dh ** -0.5
    causal = (k_pos[None, :] < q_pos[:, None])[None, None]
    lb = jnp.where(causal, jax.nn.log_sigmoid(-z), 0.0)
    suffix = lax.cumsum(lb, axis=3, reverse=True) - lb
    a = jnp.where(causal, jnp.exp(jax.nn.log_sigmoid(z) + suffix), 0.0)
    o = jnp.einsum('bhts,bshd->bthd', a.astype(v.dtype), v)
    return o.reshape(b, tq, h * dh)

def diff_attend(q, q_pos, *, k, v, k_pos, lam, gain, out_scale):
    b, tq, h, _, dh = q.shape
    sc = jnp.einsum('bthcd,bshcd->bhcts', q, k).astype(jnp.float32) * dh ** -0.5
    mask = k_pos[None, :] < chunk_end(q_pos)[:, None]
    p = jax.nn.softmax(jnp.where(mask, sc, NEG_INF), axis=-1)
    a = p[:, :, 0] - lam * p[:, :, 1]
    o = jnp.einsum('bhts,bshe->bthe', a.astype(v.dtype), v).astype(jnp.float32)
    o = o * lax.rsqrt(jnp.mean(o * o, axis=-1, keepdims=True) + NORM_EPS) * gain.astype(jnp.float32) * out_scale
    return o.astype(v.dtype).reshape(b, tq, h * 2 * dh)

def even_mixer(hn, pos, pool_hist, k_hist, v_hist, ki_hist, w_in, w_pool, pool_scale, w_out):
    b, t, _ = hn.shape
    u, q, k, v, qi, ki, wi = jnp.split(hn @ w_in, _split_points(EVEN_WIDTHS), axis=-1)
    q = rope(q.reshape(b, t, DSA_HEADS, HEAD_DIM), pos)
    k = rope(k.reshape(b, t, DSA_KV_HEADS, HEAD_DIM), pos)
    v = v.reshape(b, t, DSA_KV_HEADS, HEAD_DIM)
    qi = rope(qi.reshape(b, t, IDX_HEADS, IDX_DIM), pos)
    ki = rope(ki, pos)
    wi = wi * (IDX_HEADS * IDX_DIM) ** -0.5
    u_ext = jnp.concatenate([pool_hist, u], axis=1)
    a_out = pool_mix(u_ext, pos, w_pool, pool_scale)
    k_all = jnp.concatenate([k_hist, k], axis=1)
    v_all = jnp.concatenate([v_hist, v], axis=1)
    ki_all = jnp.concatenate([ki_hist, ki], axis=1)
    n_keys = k_all.shape[1]
    attend = functools.partial(dsa_attend, k=k_all, v=v_all, ki=ki_all,
                               k_pos=jnp.arange(n_keys, dtype=jnp.int32), n_sel=min(DSA_TOPK, n_keys // 4))
    b_out = sweep_queries(attend, (q, qi, wi), pos)
    y = jnp.concatenate([a_out, b_out], axis=-1) @ w_out
    return y, u_ext[:, -POOL_HIST:], k, v, ki

def odd_mixer(hn, pos, sbk_hist, sbv_hist, dk_hist, dv_hist, w_in, diff_lambda, diff_subln, w_out, lam_init):
    b, t, _ = hn.shape
    sq, sk, sv, dq, dk, dv = jnp.split(hn @ w_in, _split_points(ODD_WIDTHS), axis=-1)
    sq = sq.reshape(b, t, SB_HEADS, HEAD_DIM)
    sk = sk.reshape(b, t, SB_HEADS, HEAD_DIM)
    sv = sv.reshape(b, t, SB_HEADS, HEAD_DIM)
    dq = rope(dq.reshape(b, t, DIFF_HEADS, 2, HEAD_DIM), pos)
    dk = rope(dk.reshape(b, t, DIFF_HEADS, 2, HEAD_DIM), pos)
    dv = dv.reshape(b, t, DIFF_HEADS, 2 * HEAD_DIM)
    sk_all = jnp.concatenate([sbk_hist, sk], axis=1)
    sv_all = jnp.concatenate([sbv_hist, sv], axis=1)
    dk_all = jnp.concatenate([dk_hist, dk], axis=1)
    dv_all = jnp.concatenate([dv_hist, dv], axis=1)
    k_pos = jnp.arange(sk_all.shape[1], dtype=jnp.int32)
    lp = diff_lambda.astype(jnp.float32)
    lam = jnp.exp(jnp.sum(lp[0] * lp[1])) - jnp.exp(jnp.sum(lp[2] * lp[3])) + lam_init
    c_out = sweep_queries(functools.partial(sb_attend, k=sk_all, v=sv_all, k_pos=k_pos), (sq,), pos)
    d_out = sweep_queries(functools.partial(diff_attend, k=dk_all, v=dv_all, k_pos=k_pos, lam=lam,
                                            gain=diff_subln, out_scale=1.0 - lam_init), (dq,), pos)
    y = jnp.concatenate([c_out, d_out], axis=-1) @ w_out
    return y, sk, sv, dk, dv

def hier_moe(x, w_group, b_group, w_expert, b_expert, w1, w3, w2):
    n = x.shape[0]
    g_logits = (x @ w_group).astype(jnp.float32) + b_group.astype(jnp.float32)
    g_sel = jnp.argmax(g_logits, axis=-1)
    g_hot = jax.nn.one_hot(g_sel, MOE_GROUPS, dtype=jnp.float32)
    g_gate = jnp.sum(jax.nn.softmax(g_logits, axis=-1) * g_hot, axis=-1, keepdims=True)
    e_logits = jnp.einsum('nd,gde->nge', x, w_expert).astype(jnp.float32) + b_expert.astype(jnp.float32)
    e_logits = jnp.sum(e_logits * g_hot[:, :, None], axis=1)
    top_v, top_i = lax.top_k(e_logits, MOE_TOPK_INNER)
    top_w = jax.nn.softmax(top_v, axis=-1) * g_gate
    inner = jnp.sum(jax.nn.one_hot(top_i, MOE_EXPERTS_PER_GROUP, dtype=jnp.float32) * top_w[..., None], axis=1)
    gate = (g_hot[:, :, None] * inner[:, None, :]).reshape(n, MOE_EXPERTS).astype(x.dtype)
    y = jnp.zeros_like(x)
    for e in range(MOE_EXPERTS):
        hid = jax.nn.silu(x @ w1[e]) * (x @ w3[e])
        y = y + gate[:, e:e + 1] * (hid @ w2[e])
    return y

def setup_inputs(seed: int = 0) -> dict:
    key = jax.random.key(seed)
    ks = iter(jax.random.split(key, 40))

    def nrm(shape, scale=1.0):
        return jax.random.normal(next(ks), shape, jnp.float32) * scale

    def gain(shape):
        return 1.0 + nrm(shape, 0.1)

    return {
        'x_prompt': nrm((BATCH, SEQ, D_MODEL)),
        'x_sample': nrm((DEC_BATCH, DEC_SEQ, D_MODEL)),
        'cache_pool': nrm((N_EVEN, DEC_BATCH, POOL_HIST, POOL_DIM)),
        'cache_dsa_k': nrm((N_EVEN, DEC_BATCH, PAST_LEN, DSA_KV_HEADS, HEAD_DIM)),
        'cache_dsa_v': nrm((N_EVEN, DEC_BATCH, PAST_LEN, DSA_KV_HEADS, HEAD_DIM)),
        'cache_idx_k': nrm((N_EVEN, DEC_BATCH, PAST_LEN, IDX_DIM)),
        'cache_sb_k': nrm((N_ODD, DEC_BATCH, PAST_LEN, SB_HEADS, HEAD_DIM)),
        'cache_sb_v': nrm((N_ODD, DEC_BATCH, PAST_LEN, SB_HEADS, HEAD_DIM)),
        'cache_diff_k': nrm((N_ODD, DEC_BATCH, PAST_LEN, DIFF_HEADS, 2, HEAD_DIM)),
        'cache_diff_v': nrm((N_ODD, DEC_BATCH, PAST_LEN, DIFF_HEADS, 2 * HEAD_DIM)),
        'norm_mix': gain((DEPTH, D_MODEL)),
        'norm_ffn': gain((DEPTH, D_MODEL)),
        'norm_final': gain((D_MODEL,)),
        'w_in_even': nrm((N_EVEN, D_MODEL, EVEN_IN), D_MODEL ** -0.5),
        'w_pool': nrm((N_EVEN, POOL_GROUPS, POOL_GROUP_DIM, POOL_GROUP_DIM), POOL_GROUP_DIM ** -0.5),
        'pool_scale': gain((N_EVEN, POOL_DIM)),
        'w_out_even': nrm((N_EVEN, EVEN_MIX, D_MODEL), EVEN_MIX ** -0.5),
        'w_in_odd': nrm((N_ODD, D_MODEL, ODD_IN), D_MODEL ** -0.5),
        'diff_lambda': nrm((N_ODD, 4, HEAD_DIM), 0.1),
        'diff_subln': gain((N_ODD, 2 * HEAD_DIM)),
        'w_out_odd': nrm((N_ODD, ODD_MIX, D_MODEL), ODD_MIX ** -0.5),
        'moe_w_group': nrm((DEPTH, D_MODEL, MOE_GROUPS), D_MODEL ** -0.5),
        'moe_b_group': nrm((DEPTH, MOE_GROUPS), 0.01),
        'moe_w_expert': nrm((DEPTH, MOE_GROUPS, D_MODEL, MOE_EXPERTS_PER_GROUP), D_MODEL ** -0.5),
        'moe_b_expert': nrm((DEPTH, MOE_GROUPS, MOE_EXPERTS_PER_GROUP), 0.01),
        'moe_w1': nrm((DEPTH, MOE_EXPERTS, D_MODEL, MOE_HIDDEN), D_MODEL ** -0.5),
        'moe_w3': nrm((DEPTH, MOE_EXPERTS, D_MODEL, MOE_HIDDEN), D_MODEL ** -0.5),
        'moe_w2': nrm((DEPTH, MOE_EXPERTS, MOE_HIDDEN, D_MODEL), MOE_HIDDEN ** -0.5),
    }

def reference(x_prompt, x_sample, cache_pool, cache_dsa_k, cache_dsa_v, cache_idx_k, cache_sb_k, cache_sb_v,
              cache_diff_k, cache_diff_v, norm_mix, norm_ffn, norm_final, w_in_even, w_pool, pool_scale,
              w_out_even, w_in_odd, diff_lambda, diff_subln, w_out_odd, moe_w_group, moe_b_group,
              moe_w_expert, moe_b_expert, moe_w1, moe_w3, moe_w2):
    b, t, d = x_prompt.shape
    bd, td, _ = x_sample.shape
    past = cache_dsa_k.shape[2]
    dt = x_prompt.dtype
    pos_p = jnp.arange(t, dtype=jnp.int32)
    pos_s = past + jnp.arange(td, dtype=jnp.int32)
    h_p, h_s = x_prompt, x_sample
    pool_p, dsak_p, dsav_p, idxk_p, sbk_p, sbv_p, dfk_p, dfv_p = [], [], [], [], [], [], [], []
    pool_s, dsak_s, dsav_s, idxk_s, sbk_s, sbv_s, dfk_s, dfv_s = [], [], [], [], [], [], [], []
    for l in range(DEPTH):
        i = l // 2
        if l % 2 == 0:
            ew = (w_in_even[i], w_pool[i], pool_scale[i], w_out_even[i])
            y, pt, k, v, ki = even_mixer(
                rmsnorm(h_p, norm_mix[l]), pos_p, jnp.zeros((b, POOL_HIST, POOL_DIM), dt),
                jnp.zeros((b, 0, DSA_KV_HEADS, HEAD_DIM), dt), jnp.zeros((b, 0, DSA_KV_HEADS, HEAD_DIM), dt),
                jnp.zeros((b, 0, IDX_DIM), dt), *ew)
            h_p = h_p + y
            pool_p.append(pt); dsak_p.append(k); dsav_p.append(v); idxk_p.append(ki)
            y, pt, k, v, ki = even_mixer(rmsnorm(h_s, norm_mix[l]), pos_s, cache_pool[i], cache_dsa_k[i],
                                         cache_dsa_v[i], cache_idx_k[i], *ew)
            h_s = h_s + y
            pool_s.append(pt); dsak_s.append(k); dsav_s.append(v); idxk_s.append(ki)
        else:
            lam_init = 0.8 - 0.6 * math.exp(-0.3 * l)
            ow = (w_in_odd[i], diff_lambda[i], diff_subln[i], w_out_odd[i], lam_init)
            y, sk, sv, dk, dv = odd_mixer(
                rmsnorm(h_p, norm_mix[l]), pos_p,
                jnp.zeros((b, 0, SB_HEADS, HEAD_DIM), dt), jnp.zeros((b, 0, SB_HEADS, HEAD_DIM), dt),
                jnp.zeros((b, 0, DIFF_HEADS, 2, HEAD_DIM), dt), jnp.zeros((b, 0, DIFF_HEADS, 2 * HEAD_DIM), dt), *ow)
            h_p = h_p + y
            sbk_p.append(sk); sbv_p.append(sv); dfk_p.append(dk); dfv_p.append(dv)
            y, sk, sv, dk, dv = odd_mixer(rmsnorm(h_s, norm_mix[l]), pos_s, cache_sb_k[i], cache_sb_v[i],
                                          cache_diff_k[i], cache_diff_v[i], *ow)
            h_s = h_s + y
            sbk_s.append(sk); sbv_s.append(sv); dfk_s.append(dk); dfv_s.append(dv)
        mw = (moe_w_group[l], moe_b_group[l], moe_w_expert[l], moe_b_expert[l], moe_w1[l], moe_w3[l], moe_w2[l])
        h_p = h_p + hier_moe(rmsnorm(h_p, norm_ffn[l]).reshape(b * t, d), *mw).reshape(b, t, d)
        h_s = h_s + hier_moe(rmsnorm(h_s, norm_ffn[l]).reshape(bd * td, d), *mw).reshape(bd, td, d)
    y_prompt = rmsnorm(h_p, norm_final)
    y_sample = rmsnorm(h_s, norm_final)
    return (y_prompt, y_sample,
            jnp.stack(pool_p), jnp.stack(dsak_p), jnp.stack(dsav_p), jnp.stack(idxk_p),
            jnp.stack(sbk_p), jnp.stack(sbv_p), jnp.stack(dfk_p), jnp.stack(dfv_p),
            jnp.stack(pool_s), jnp.stack(dsak_s), jnp.stack(dsav_s), jnp.stack(idxk_s),
            jnp.stack(sbk_s), jnp.stack(sbv_s), jnp.stack(dfk_s), jnp.stack(dfv_s))


_drawn_inputs = setup_inputs


def setup_inputs(seed=0):
    import zlib

    import numpy as np

    out = dict(_drawn_inputs(seed))
    spreads = {}
    factors = {'moe_b_expert': 3.501}
    for name, (base, spread) in spreads.items():
        noise = np.random.default_rng([zlib.crc32(name.encode()), seed]).standard_normal(out[name].shape)
        drawn = base * np.exp(spread * noise) if base else spread * noise
        out[name] = __import__('jax').numpy.asarray(drawn.astype(out[name].dtype))
    for name, factor in factors.items():
        out[name] = (out[name] * factor).astype(out[name].dtype)
    return out
```

```python
import concourse.bass as bass
from concourse import mybir
from contextlib import ExitStack

F32 = mybir.dt.float32
ALU = mybir.AluOpType
ACT = mybir.ActivationFunctionType
AX_X = mybir.AxisListType.X

P = 128
DM = 1024
KC = DM // P
SEQ, DEC, PAST = 512, 32, 256
NT = 5
ROWS = [P] * 4 + [DEC]
NTOK = SEQ + DEC
NKEY = SEQ + PAST + DEC
HD = 64
CHUNK = 64
HIST = 15
WINDOWS = (2, 4, 8, 16)
UEXT = HIST + SEQ + HIST + DEC
USAM = HIST + SEQ + HIST
PROMPT_SEL, SAMPLE_SEL = 128, 72
KIW = 68
NE = 16
FH = 512
EPS = 1e-6
NEG = -1e30
TAKEN = -3e38
LAM_INIT = 0.8 - 0.6 * 0.7408182206817179

C_COS, C_SIN, C_ID, C_CHUNK, C_CAUSAL, C_RCNT, C_J = 0, 160, 320, 448, 960, 1472, 1536
C_N = 1540

S_U, S_Q, S_KV = 0, 1, 2
SB_K, SB_V, SB_Q = 0, 1, 2
DF_K, DF_V, DF_Q = 4, 0, 1
OUT_EVEN, OUT_ODD = (0, 4), (2, 4)
W1, W3, W2 = (1, 3), (2, 5), (0, 4)


def tok(t):
    return slice(P * t, P * t + ROWS[t])


def keys_at(t):
    return (0, P * (t + 1), P * t) if t < 4 else (SEQ, PAST + DEC, SEQ + PAST)


def key_blocks(t):
    return [(b, P) for b in range(t + 1)] if t < 4 else [(4, P), (5, P), (6, DEC)]


def own_block(t):
    return t if t < 4 else 6


HEADS = {"dsa": 8, "sb": 8, "diff": 4}
LAG = {"dsa": 1, "sb": 2, "diff": 2}
TURN = {"dsa": "act", "sb": "dve", "diff": "act"}


def schedule(mech):
    steps = [("P", 0)]
    for t in range(NT):
        if t + 1 < NT:
            steps.append(("P", t + 1))
        if t > 0:
            steps.append(("O", t - 1))
        steps.append(("A", t))
        if mech == "dsa" and t < 4:
            steps.append(("U", t))
    return steps + [("O", NT - 1)]


def bank_plan():
    plan = []

    def norm(n):
        for t in range(NT):
            for j in range(2):
                plan.append((("xT", n, t, j), "dve"))

    def attention(mech):
        for kind, t in schedule(mech):
            if kind == "P":
                if t == NT - 1:
                    for b in range(2):
                        plan.append(((mech, "cache", b), "act"))
                if mech == "dsa":
                    plan.append(((mech, "kv", t), "dve"))
                    plan.append(((mech, "ki", t), "dve"))
                    plan.append(((mech, "q", t), "dve"))
                    plan.append(((mech, "kT", t), "act"))
                    plan.append(((mech, "qiT", t), "act"))
                    plan.append(((mech, "qT", t), "act"))
                    for h in range(4):
                        plan.append(((mech, "ix", t, h), "act"))
                else:
                    plan.append(((mech, "k", t), "act" if mech == "sb" else "dve"))
                    plan.append(((mech, "v", t), "act"))
                    plan.append(((mech, "q", t), "dve"))
                    plan.append(((mech, "kT", t), "act"))
                    plan.append(((mech, "qT", t), "act"))
            elif kind == "A":
                lag = LAG[mech]
                for step in range(HEADS[mech] + lag):
                    if step < HEADS[mech]:
                        for c in range(2 if mech == "diff" else 1):
                            plan.append(((mech, "s", t, step, c), "dve"))
                    if step >= lag:
                        plan.append(((mech, "pT", t, step - lag), TURN[mech]))
            elif kind == "O":
                plan.append(((mech, "oT", t), "act"))
            elif kind == "U":
                plan.append(((mech, "a", t), "act"))
                plan.append(((mech, "as", t), "act"))

    def project_out(layer):
        for t in range(NT):
            for j in range(2):
                plan.append((("y", layer, t, j), "dve"))

    norm(0)
    for f in range(4):
        plan.append((("u", f), "act"))
    plan.append((("us",), "act"))
    plan.append((("hist",), "act"))
    plan.append((("pool_p",), "act"))
    plan.append((("pool_s",), "act"))
    attention("dsa")
    project_out(0)
    norm(1)
    plan.append((("router", 0), "dve"))
    norm(2)
    attention("sb")
    attention("diff")
    project_out(1)
    norm(3)
    plan.append((("router", 1), "dve"))
    return plan


def stream_kernel(nc, x_prompt, x_sample, cache_pool, cache_dsa_k, cache_dsa_v, cache_idx_k, cache_sb_k,
                  cache_sb_v, cache_diff_k, cache_diff_v, norm_mix, norm_ffn, norm_final, w_in_even, w_pool,
                  pool_scale, w_out_even, w_in_odd, diff_lambda, diff_subln, w_out_odd, moe_w_group,
                  moe_b_group, moe_w_expert, moe_b_expert, moe_w1, moe_w3, moe_w2, constants,
                  y_prompt, y_sample, pool_p, dsak_p, dsav_p, idxk_p, sbk_p, sbv_p, dfk_p, dfv_p,
                  pool_s, dsak_s, dsav_s, idxk_s, sbk_s, sbv_s, dfk_s, dfv_s):
    plan = bank_plan()
    NB = 6
    number = {key: i for i, (key, _) in enumerate(plan)}
    reader = dict(plan)
    rank, last_rank = {}, {"act": 0, "dve": 0}
    for key, who in plan:
        last_rank[who] += 1
        rank[key] = last_rank[who]

    ctx = ExitStack()
    with ctx:
        def sb(name, shape, dt=F32):
            return ctx.enter_context(nc.sbuf_tensor(name, shape, dt))

        def sem(name):
            return ctx.enter_context(nc.semaphore(name))

        h = sb("h", [P, NT, DM])
        normed = sb("normed", [P, NT * DM])
        xT = sb("xT", [P, KC, NTOK])
        slot = sb("slot", [P, 6, 4096])
        const = sb("const", [P, C_N])
        params = sb("params", [P, 768])
        stats = sb("stats", [P, 640])
        arena = sb("arena", [P, 11040])

        xn = normed[:, :].rearrange("p (t d) -> p t d", t=NT)
        mixT = normed[:, 0:8 * NTOK].rearrange("p (f n) -> p f n", f=8)
        spare = normed[:, 8 * NTOK:NT * DM]
        cos = const[:, C_COS:C_COS + 160].rearrange("p (t e) -> p t e", t=NT)
        sin = const[:, C_SIN:C_SIN + 160].rearrange("p (t e) -> p t e", t=NT)
        ident = const[:, C_ID:C_ID + P]

        g_norm = params[:, 0:32].rearrange("p (n k) -> p n k", n=4)
        w_router = params[:, 32:352].rearrange("p (l k n) -> p l k n", l=2, k=KC)
        b_router = params[:, 352:392].rearrange("p (l n) -> p l n", l=2)
        scale_pool = params[:, 392:396]
        gain_diff = params[:, 396:397]
        gain_out = params[:, 397:398]
        lam_in = params[:, 400:656]
        lam_dot = params[:, 656:658]
        lam_exp = params[:, 658:660]
        lam = params[:, 660:661]
        lam_tmp = params[:, 664:728]

        ssq = stats[:, 0:25].rearrange("p (n t) -> p n t", n=5)
        mean = stats[:, 25:50].rearrange("p (n t) -> p n t", n=5)
        std = stats[:, 50:75].rearrange("p (n t) -> p n t", n=5)
        rstd = stats[:, 75:100].rearrange("p (n t) -> p n t", n=5)
        least = stats[:, 100:116].rearrange("p (r c) -> p r c", r=8)
        rowsum = stats[:, 116:132].rearrange("p (r c) -> p r c", r=8)
        rinv = stats[:, 132:148].rearrange("p (r c) -> p r c", r=8)
        top8 = stats[:, 148:156]
        w_idx = stats[:, 156:164].rearrange("p (r c) -> p r c", r=2)
        osq = stats[:, 164:168]
        oms = stats[:, 168:172]
        oln = stats[:, 172:176]
        ors = stats[:, 176:180]
        logits = stats[:, 180:280].rearrange("p (t n) -> p t n", t=NT)
        gate = stats[:, 280:360].rearrange("p (t n) -> p t n", t=NT)
        route = stats[:, 360:640]

        r_exp = route[:, 0:25]
        r_arg = route[:, 25:50]

        at = 0

        def area(n):
            nonlocal at
            at += n
            return arena[:, at - n:at]

        kT = area(4 * NKEY).rearrange("p (f n) -> p f n", f=4)
        values = area(7 * 512)
        qT = area(1024).rearrange("p (r f n) -> p r f n", r=2, f=4)
        rows = area(1152)
        ropeA = area(512)
        ropeB = area(512)
        lo, hi = slot[:, 3, :], slot[:, 5, :]
        crow = lo[:, 0:1024].rearrange("p (b n) -> p b n", b=2)
        score = lo[:, 1024:2048].rearrange("p (r n) -> p r n", r=2)
        prob = lo[:, 2048:3072].rearrange("p (r n) -> p r n", r=2)
        probT = lo[:, 3072:4096].rearrange("p (r b n) -> p r b n", r=2, b=4)
        orow = hi[:, 0:1024].rearrange("p (r n) -> p r n", r=2)
        idxrel = hi[:, 1024:1536]
        idxacc = hi[:, 1536:2048]
        pooled = hi[:, 2048:2560]
        pooled_s = spare[:, UEXT:UEXT + DEC]
        selected = hi[:, 2560:3584].rearrange("p (r n) -> p r n", r=2)
        wpool = hi[:, 3584:4096].rearrange("p (g n) -> p g n", g=4)
        kiw = area(KC * KIW).rearrange("p (k n) -> p k n", k=KC)
        qiT = area(512).rearrange("p (r f n) -> p r f n", r=2, f=2)
        uT = values[:, 896:896 + 4 * UEXT].rearrange("p (g n) -> p g n", g=4)
        sumA = spare[:, 0:UEXT]
        sumB = kT[:, 3, 0:UEXT]
        logp = hi[:, 1024:2048].rearrange("p (r n) -> p r n", r=2)
        tail = hi[:, 2048:3072].rearrange("p (r n) -> p r n", r=2)
        expo = hi[:, 1024:3072].rearrange("p (r n) -> p r n", r=4)
        odd_junk = hi[:, 3072:3584]
        vdsa = values[:, 0:896].rearrange("p (b n) -> p b n", b=7)
        vodd = values.rearrange("p (b n) -> p b n", b=7)
        hid = arena[:, 0:4 * NTOK].rearrange("p (m n) -> p m n", m=4)
        silu = arena[:, 4 * NTOK:6 * NTOK].rearrange("p (r s n) -> p r s n", r=2, s=2)
        junk = xT[:, 0:2, :].rearrange("p k n -> p (k n)")[:, 0:DM]
        fin = normed[:, :].rearrange("p (t d) -> p t d", t=NT)
        gfin = slot[:, 0, 0:DM]
        histrow = ropeA
        poolout = ropeB

        bank = ctx.enter_context(nc.psum_tensor("bank", [P, 8, 512], F32))

        x_in = sem("x_in")
        const_in = sem("const_in")
        small_in = sem("small_in")
        slot_in = [sem(f"slot{s}_in") for s in range(6)]
        kiw_in = sem("kiw_in")
        wpool_in = sem("wpool_in")
        hist_in = sem("hist_in")
        krow_in = sem("krow_in")
        vrow_in = sem("vrow_in")
        w13_in = [sem("even_w13_in"), sem("odd_w13_in")]
        w2_in = [sem("even_w2_in"), sem("odd_w2_in")]
        gfin_in = sem("gfin_in")
        bank_filled = sem("bank_filled")
        bank_read = {"act": sem("bank_read_act"), "dve": sem("bank_read_dve")}
        out_filled = sem("out_filled")
        out_read = sem("out_read")
        squared = sem("squared")
        mean_ready = sem("mean_ready")
        std_ready = sem("std_ready")
        xn_ready = sem("xn_ready")
        zeros_set = sem("zeros_set")
        rope_out = sem("rope_out")
        index_ready = sem("index_ready")
        soft_ready = sem("soft_ready")
        tail_ready = sem("tail_ready")
        expo_in = sem("expo_in")
        exp_done = sem("exp_done")
        prob_ready = sem("prob_ready")
        osq_ready = sem("osq_ready")
        ors_ready = sem("ors_ready")
        sums_ready = sem("sums_ready")
        pooled_ready = sem("pooled_ready")
        lam_dots = sem("lam_dots")
        lam_exps = sem("lam_exps")
        out_rows = sem("out_rows")
        out_vals = sem("out_vals")
        out_pool = sem("out_pool")
        out_y = sem("out_y")
        route_in = sem("route_in")
        route_exp = sem("route_exp")
        moe_g = sem("moe_g")
        moe_u = sem("moe_u")
        moe_y = sem("moe_y")
        silu_done = sem("silu_done")
        hid_done = sem("hid_done")
        y_added = sem("y_added")
        fin_ready = sem("fin_ready")
        act_step = sem("act_step")
        dve_step = sem("dve_step")
        pool_step = sem("pool_step")

        block = ctx.enter_context(nc.Block())

        def filled(eng, key):
            eng.wait_ge(bank_filled, number[key] + 1)
            return bank[:, number[key] % NB, :]

        def taken(eng, key):
            eng.wait_ge(bank_read[reader[key]], rank[key])

        MECHS = ("dsa", "sb", "diff")
        tiles_before = {m: NT * i for i, m in enumerate(MECHS)}
        heads_before = {"dsa": 0, "sb": 8 * NT, "diff": 16 * NT}
        maps_before = {"dsa": 0, "sb": 8 * NT, "diff": 16 * NT}
        scores_before = maps_before

        def head_no(mech, t, hd):
            return heads_before[mech] + t * HEADS[mech] + hd

        def map_no(mech, t, hd, c):
            n = 2 if mech == "diff" else 1
            return maps_before[mech] + (t * HEADS[mech] + hd) * n + c

        def rope_no(mech, t, part):
            return (0 if mech == "dsa" else 2 * NT) + 2 * t + part

        def rows2d(ap):
            return ap.rearrange("a b s g d -> (a b s) (g d)")

        @block.sync
        def _(sp):
            sp.dma_start(h[:, 0:4, :], x_prompt[0].rearrange("(t p) d -> p t d", p=P)).then_inc(x_in, 16)
            sp.dma_start(h[0:DEC, 4, :], x_sample[0]).then_inc(x_in, 16)
            sp.dma_start(const[:, :], constants).then_inc(const_in, 16)
            for n, g in enumerate((norm_mix[0], norm_ffn[0], norm_mix[1], norm_ffn[1])):
                sp.dma_start(g_norm[:, n, :], g.rearrange("(p k) -> p k", k=KC)).then_inc(small_in, 16)
            for f in range(1):
                sp.dma_start(slot[:, S_U, :].rearrange("p (k n) -> p k n", k=KC),
                             w_in_even[0].rearrange("(p k) n -> p k n", k=KC)[:, :, 0:512])\
                  .then_inc(slot_in[S_U], 16)
            sp.dma_start(histrow[0:HIST, :], cache_pool[0, 0]).then_inc(hist_in, 16)
            sp.dma_start(slot[:, S_KV, :].rearrange("p (k n) -> p k n", k=KC),
                         w_in_even[0].rearrange("(p k) n -> p k n", k=KC)[:, :, 1024:1536])\
              .then_inc(slot_in[S_KV], 16)
            sp.dma_start(kiw, w_in_even[0].rearrange("(p k) n -> p k n", k=KC)[:, :, 1536:1536 + KIW])\
              .then_inc(kiw_in, 16)
            sp.dma_start(slot[:, S_Q, :].rearrange("p (k n) -> p k n", k=KC),
                         w_in_even[0].rearrange("(p k) n -> p k n", k=KC)[:, :, 512:1024])\
              .then_inc(slot_in[S_Q], 16)
            sp.dma_start(wpool, w_pool[0].rearrange("g c n -> c g n")).then_inc(wpool_in, 16)
            with nc.allow_non_contiguous_dma(reason="a few columns of parameters"):
                sp.dma_start(scale_pool, pool_scale[0].rearrange("(g p) -> p g", p=P)).then_inc(small_in, 16)
                sp.dma_start(gain_diff, diff_subln[0].rearrange("(p a) -> p a", a=1)).then_inc(small_in, 16)
                for l in range(2):
                    sp.dma_start(w_router[:, l, :, 0:4], moe_w_group[l].rearrange("(p k) n -> p k n", k=KC))\
                      .then_inc(small_in, 16)
                    for g in range(4):
                        sp.dma_start(w_router[:, l, :, 4 + 4 * g:8 + 4 * g],
                                     moe_w_expert[l, g].rearrange("(p k) n -> p k n", k=KC))\
                          .then_inc(small_in, 16)
            for l in range(2):
                sp.dma_start(b_router[:, l, 0:4], moe_b_group[l].partition_broadcast(P)).then_inc(small_in, 16)
                sp.dma_start(b_router[:, l, 4:20], moe_b_expert[l].rearrange("g n -> (g n)")
                             .partition_broadcast(P)).then_inc(small_in, 16)
            sp.dma_start(lam_in, diff_lambda[0].rearrange("a n -> (a n)").partition_broadcast(P))\
              .then_inc(small_in, 16)
            ck = crow[:, :, 0:256].rearrange("p b (g u d) -> p b g u d", g=2, u=2)
            for b in range(2):
                for u in range(2):
                    sp.dma_start(ck[:, b, :, u, :], cache_dsa_k[0, 0, P * b:P * b + P]).then_inc(krow_in, 16)
                    sp.dma_start(crow[:, b, 256 + HD * u:256 + HD * u + HD],
                                 cache_idx_k[0, 0, P * b:P * b + P]).then_inc(krow_in, 16)
                sp.dma_start(vdsa[:, 4 + b, :], cache_dsa_v[0, 0, P * b:P * b + P]
                             .rearrange("p g d -> p (g d)")).then_inc(vrow_in, 16)

            def w_out_load(w, slots, waits):
                for j in range(2):
                    waits[j]()
                    sp.dma_start(slot[:, slots[j], :].rearrange("p (k n) -> p k n", k=4),
                                 w[0].rearrange("(k p) n -> p k n", p=P)[:, 4 * j:4 * j + 4, :])\
                      .then_inc(slot_in[slots[j]], 16)

            w_out_load(w_out_even, OUT_EVEN, (lambda: sp.wait_ge(bank_filled, number[("us",)] + 1),
                                              lambda: None))

            def expert_loads(l, e, par, first):
                for w, s, arrived, k in ((moe_w1, W1, w13_in, KC), (moe_w3, W3, w13_in, KC),
                                         (moe_w2, W2, w2_in, 4)):
                    if first:
                        first(s[par])
                    src = w[l, e]
                    src = src.rearrange("(p k) n -> p k n", k=KC) if k == KC else \
                        src.rearrange("(k p) n -> p k n", p=P)
                    sp.dma_start(slot[:, s[par], :].rearrange("p (k n) -> p k n", k=k), src)\
                      .then_inc(arrived[par], 16)

            def experts(l, first):
                expert_loads(l, 0, 0, first)
                expert_loads(l, 1, 1, first)
                with sp.Fori(0, NE // 2 - 1) as i:
                    for par in range(2):
                        sp.wait_ge(moe_y, (2 * i + par + 1) * NT + l * NE * NT)
                        expert_loads(l, 2 * i + 2 + par, par, None)

            def mixer_left(layer, mech, freed):
                def wait(s):
                    key = freed.get(s)
                    sp.wait_ge(bank_filled, number[key] + 1)
                    if s in (3, 5):
                        sp.wait_ge(out_read, tiles_before[mech] + NT)
                        taken(sp, (mech, "oT", NT - 1))
                return wait

            left = ("y", 0, NT - 1, 1)
            experts(0, mixer_left(0, "dsa", {1: ("dsa", "q", 4), 2: ("dsa", "kv", 4), 0: left, 4: left,
                                             3: left, 5: left}))

            def odd_load(s, c, then):
                if then:
                    sp.wait_ge(bank_filled, number[then] + 1)
                sp.dma_start(slot[:, s, :].rearrange("p (k n) -> p k n", k=KC),
                             w_in_odd[0].rearrange("(p k) n -> p k n", k=KC)[:, :, 512 * c:512 * c + 512])\
                  .then_inc(slot_in[s], 16)

            sp.wait_ge(moe_y, (NE - 1) * NT)
            odd_load(SB_K, 1, None)
            odd_load(SB_V, 2, None)
            odd_load(SB_Q, 0, None)
            sp.wait_ge(moe_y, NE * NT)
            odd_load(DF_K, 4, None)

            def cache_load(k, v, mech):
                for b in range(2):
                    src_k, src_v = k[0, 0, P * b:P * b + P], v[0, 0, P * b:P * b + P]
                    src_k = src_k.rearrange("p g d -> p (g d)") if mech == "sb" else \
                        src_k.rearrange("p g c d -> p (g c d)")
                    sp.dma_start(crow[:, b, :], src_k).then_inc(krow_in, 16)
                    sp.dma_start(vodd[:, 4 + b, :], src_v.rearrange("p g d -> p (g d)")).then_inc(vrow_in, 16)

            sp.wait_ge(y_added, 1 + NE * NT)
            cache_load(cache_sb_k, cache_sb_v, "sb")
            odd_load(DF_V, 5, ("sb", "k", 4))
            odd_load(DF_Q, 3, ("sb", "v", 4))
            def after_sb():
                sp.wait_ge(bank_filled, number[("sb", "q", 4)] + 1)

            def after_diff_k():
                sp.wait_ge(out_filled, head_no("sb", 4, 7) + 1)
                cache_load(cache_diff_k, cache_diff_v, "diff")
                sp.wait_ge(bank_filled, number[("diff", "k", 4)] + 1)

            w_out_load(w_out_odd, OUT_ODD, (after_sb, after_diff_k))
            left = ("y", 1, NT - 1, 1)
            experts(1, mixer_left(1, "diff", {1: ("diff", "q", 4), 0: ("diff", "v", 4), 2: left, 4: left,
                                              3: left, 5: left}))
            sp.wait_ge(moe_y, 2 * NE * NT - NT)
            sp.dma_start(gfin, norm_final.partition_broadcast(P)).then_inc(gfin_in, 16)
            for t in range(NT):
                sp.wait_ge(fin_ready, t + 1)
                dst = y_prompt[0, P * t:P * t + P, :] if t < 4 else y_sample[0]
                sp.dma_start(dst, fin[0:ROWS[t], t, :]).then_inc(out_y, 16)
            sp.wait_ge(out_y, 16 * NT)
            sp.wait_ge(out_rows, 16 * (2 + 1 + 1) * NT)
            sp.wait_ge(out_vals, 16 * 3 * NT)
            sp.wait_ge(out_pool, 32)

        @block.tensor
        def _(pe):
            turn = [0]

            def fill(key):
                i = number[key]
                assert turn[0] == i, (key, plan[turn[0]])
                turn[0] += 1
                if i >= NB:
                    taken(pe, plan[i - NB][0])
                return bank[:, i % NB, :]

            def weights(s, n=KC):
                return slot[:, s, :].rearrange("p (k n) -> p k n", k=n)

            def turn_norm(n):
                for t in range(NT):
                    pe.wait_ge(xn_ready, NT * n + t + 1)
                    r = ROWS[t]
                    src = xn[0:r, t, :].rearrange("r (p k) -> r k p", k=KC)
                    for j in range(2):
                        b = fill(("xT", n, t, j))
                        for k in range(4):
                            last = nc.tensor.transpose(b[:, P * k:P * k + r], src[:, 4 * j + k, :],
                                                       ident[0:r, 0:r])
                        last.then_inc(bank_filled, 1)

            def xT_ready(n, t):
                taken(pe, ("xT", n, t, 1))

            def project(key, t, w, n):
                b = fill(key)
                for k in range(KC):
                    last = nc.tensor.matmul(b[0:ROWS[t], 0:n], xT[:, k, tok(t)], w[:, k, 0:n],
                                            start=(k == 0), stop=(k == KC - 1))
                last.then_inc(bank_filled, 1)

            def transposes(key, srcs, r):
                b = fill(key)
                for i, s in enumerate(srcs):
                    last = nc.tensor.transpose(b[0:s.shape[1], P * i:P * i + r], s, ident[0:r, 0:r])
                last.then_inc(bank_filled, 1)

            pe.wait_ge(const_in, 16)
            turn_norm(0)
            pe.wait_ge(slot_in[S_U], 16)
            for f in range(4):
                b = fill(("u", f))
                if f == 0:
                    for t in range(NT):
                        xT_ready(0, t)
                for k in range(KC):
                    last = nc.tensor.matmul(b[:, :], weights(S_U)[:, k, P * f:P * f + P], xT[:, k, 0:SEQ],
                                            start=(k == 0), stop=(k == KC - 1))
                last.then_inc(bank_filled, 1)
            b = fill(("us",))
            for f in range(4):
                for k in range(KC):
                    last = nc.tensor.matmul(b[:, DEC * f:DEC * f + DEC], weights(S_U)[:, k, P * f:P * f + P],
                                            xT[:, k, SEQ:NTOK], start=(k == 0), stop=(k == KC - 1))
            last.then_inc(bank_filled, 1)
            b = fill(("hist",))
            pe.wait_ge(hist_in, 16)
            for f in range(4):
                last = nc.tensor.transpose(b[:, 16 * f:16 * f + HIST], histrow[0:HIST, P * f:P * f + P],
                                           ident[0:HIST, 0:HIST])
            last.then_inc(bank_filled, 1)
            for key, c in ((("pool_p",), SEQ), (("pool_s",), UEXT - HIST)):
                b = fill(key)
                for f in range(4):
                    taken(pe, ("u", f))
                taken(pe, ("us",))
                for f in range(4):
                    last = nc.tensor.transpose(b[0:HIST, P * f:P * f + P], uT[:, f, c:c + HIST], ident)
                last.then_inc(bank_filled, 1)

            def step_P(mech, t):
                r = ROWS[t]
                if t == NT - 1:
                    for b in range(2):
                        pe.wait_ge(krow_in, {"dsa": 128, "sb": 160, "diff": 192}[mech])
                        n = 3 if mech == "dsa" else 4
                        transposes((mech, "cache", b), [crow[:, b, P * i:P * i + P] for i in range(n)], P)
                own = keys_at(t)[2]
                if mech == "dsa":
                    if t == 0:
                        pe.wait_ge(slot_in[S_KV], 16)
                        pe.wait_ge(slot_in[S_Q], 16)
                        pe.wait_ge(kiw_in, 16)
                    project((mech, "kv", t), t, weights(S_KV), 512)
                    project((mech, "ki", t), t, kiw, KIW)
                    project((mech, "q", t), t, weights(S_Q), 512)
                    pe.wait_ge(rope_out, rope_no(mech, t, 0) + 1)
                    transposes((mech, "kT", t), [rows[0:r, P * i:P * i + P] for i in (0, 1, 4)], r)
                    transposes((mech, "qiT", t), [rows[0:r, P * i:P * i + P] for i in (2, 3)], r)
                    pe.wait_ge(rope_out, rope_no(mech, t, 1) + 1)
                    transposes((mech, "qT", t), [rows[0:r, P * i:P * i + P] for i in (5, 6, 7, 8)], r)
                    k0, nk, _ = keys_at(t)
                    for hd in range(4):
                        b = fill((mech, "ix", t, hd))
                        if hd == 0:
                            taken(pe, (mech, "qiT", t))
                        o = HD * (hd % 2)
                        nc.tensor.matmul(b[0:r, 0:nk], qiT[o:o + HD, t % 2, hd // 2, 0:r],
                                         kT[o:o + HD, 2, k0:k0 + nk], start=True, stop=True)\
                          .then_inc(bank_filled, 1)
                    return
                sk, sv, sq = (SB_K, SB_V, SB_Q) if mech == "sb" else (DF_K, DF_V, DF_Q)
                n = 2 if mech == "diff" else 1
                if t == 0:
                    for s in (sk, sv, sq):
                        pe.wait_ge(slot_in[s], slot_count(s, mech))
                    if mech == "sb":
                        for tt in range(NT):
                            xT_ready(2, tt)
                project((mech, "k", t), t, weights(sk), 512)
                project((mech, "v", t), t, weights(sv), 512)
                project((mech, "q", t), t, weights(sq), 512)
                if mech == "sb":
                    taken(pe, (mech, "k", t))
                else:
                    pe.wait_ge(rope_out, rope_no(mech, t, 0) + 1)
                transposes((mech, "kT", t), [rows[0:r, P * i:P * i + P] for i in range(4)], r)
                if mech == "sb":
                    taken(pe, (mech, "q", t))
                else:
                    pe.wait_ge(rope_out, rope_no(mech, t, 1) + 1)
                transposes((mech, "qT", t), [rows[0:r, P * i:P * i + P] for i in range(4, 8)], r)

            def step_A(mech, t):
                r, lag = ROWS[t], LAG[mech]
                k0, nk, _ = keys_at(t)
                tile = tiles_before[mech] + t
                out = bank[:, NB + tile % 2, :]
                blocks = key_blocks(t)
                for step in range(HEADS[mech] + lag + 1):
                    if step < HEADS[mech]:
                        if step == 0:
                            taken(pe, (mech, "qT", t))
                            taken(pe, (mech, "kT", t))
                            if t == NT - 1:
                                taken(pe, (mech, "cache", 1))
                        for c in range(2 if mech == "diff" else 1):
                            b = fill((mech, "s", t, step, c))
                            if mech == "diff":
                                o, f, kf = HD * c, step, step
                            else:
                                o, f = HD * (step % 2), step // 2
                                kf = step // 4 if mech == "dsa" else f
                            nc.tensor.matmul(b[0:r, 0:nk], qT[o:o + HD, t % 2, f, 0:r],
                                             kT[o:o + HD, kf, k0:k0 + nk], start=True, stop=True)\
                              .then_inc(bank_filled, 1)
                    hd = step - lag
                    if 0 <= hd < HEADS[mech]:
                        n = head_no(mech, t, hd)
                        b = fill((mech, "pT", t, hd))
                        pe.wait_ge(prob_ready, n + 1)
                        for i, (_, kr) in enumerate(blocks):
                            last = nc.tensor.transpose(b[0:kr, P * i:P * i + r],
                                                       prob[0:r, n % 2, P * i:P * i + kr], ident[0:r, 0:r])
                        last.then_inc(bank_filled, 1)
                    hd = step - lag - 1
                    if 0 <= hd < HEADS[mech]:
                        n = head_no(mech, t, hd)
                        if hd == 0:
                            if tile >= 2:
                                pe.wait_ge(out_read, tile - 1)
                            if mech != "dsa":
                                taken(pe, (mech, "v", t))
                            if t == NT - 1:
                                pe.wait_ge(vrow_in, {"dsa": 32, "sb": 64, "diff": 96}[mech])
                        taken(pe, (mech, "pT", t, hd))
                        vals, w, c = {"dsa": (vdsa, HD, HD * (hd // 4)), "sb": (vodd, HD, HD * hd),
                                      "diff": (vodd, P, P * hd)}[mech]
                        for i, (vb, kr) in enumerate(blocks):
                            last = nc.tensor.matmul(out[0:r, w * hd:w * hd + w], probT[0:kr, n % 2, i, 0:r],
                                                    vals[0:kr, vb, c:c + w], start=(i == 0),
                                                    stop=(i == len(blocks) - 1))
                        last.then_inc(out_filled, 1)

            def step_O(mech, t):
                tile = tiles_before[mech] + t
                pe.wait_ge(out_read, tile + 1)
                r = ROWS[t]
                transposes((mech, "oT", t), [orow[0:r, tile % 2, P * i:P * i + P] for i in range(4)], r)

            def step_U(g):
                if g == 0:
                    pe.wait_ge(wpool_in, 16)
                pe.wait_ge(pooled_ready, g + 1)
                for key, rhs, n in ((("dsa", "a", g), pooled, SEQ), (("dsa", "as", g), pooled_s, DEC)):
                    b = fill(key)
                    nc.tensor.matmul(b[:, 0:n], wpool[:, g, :], rhs,
                                     start=True, stop=True).then_inc(bank_filled, 1)

            def attention(mech):
                for kind, t in schedule(mech):
                    if kind == "P":
                        step_P(mech, t)
                    elif kind == "A":
                        step_A(mech, t)
                    elif kind == "O":
                        step_O(mech, t)
                    else:
                        step_U(t)

            def slot_count(s, mech):
                loads = {"dsa": (0, 1, 2), "out0": (0, 4), "sb": (0, 1, 2), "diff": (4, 0, 1), "out1": (2, 4)}
                n = 0
                for name, slots in loads.items():
                    n += slots.count(s)
                    if name == mech:
                        return 16 * n

            def project_out(layer, slots):
                for s in slots:
                    pe.wait_ge(slot_in[s], slot_count(s, f"out{layer}"))
                mech = "dsa" if layer == 0 else "diff"
                if layer == 1:
                    taken(pe, ("sb", "oT", NT - 1))
                taken(pe, (mech, "oT", NT - 1))
                for t in range(NT):
                    for j in range(2):
                        b = fill(("y", layer, t, j))
                        for k in range(KC):
                            w = weights(slots[k // 4], 4)
                            last = nc.tensor.matmul(b[0:ROWS[t], :], mixT[:, k, tok(t)],
                                                    w[:, k % 4, 512 * j:512 * j + 512],
                                                    start=(k == 0), stop=(k == KC - 1))
                        last.then_inc(bank_filled, 1)

            def router(l):
                b = fill(("router", l))
                for t in range(NT):
                    xT_ready(2 * l + 1, t)
                    for k in range(KC):
                        last = nc.tensor.matmul(b[0:ROWS[t], 20 * t:20 * t + 20], xT[:, k, tok(t)],
                                                w_router[:, l, k, :], start=(k == 0), stop=(k == KC - 1))
                last.then_inc(bank_filled, 1)

            def experts(l):
                for who in ("act", "dve"):
                    pe.wait_ge(bank_read[who], max(rank[k] for k, v in plan[0:number[("router", l)] + 1]
                                                   if v == who))
                pe.wait_ge(out_read, NT if l == 0 else 3 * NT)
                with pe.Fori(0, NE // 2) as i:
                    for par in range(2):
                        expert_body(l, 2 * i + (l * NE + par), i + l * (NE // 2), par)

            def expert_body(l, n, pairs, par):
                pe.wait_ge(w13_in[par], 32 * pairs + 32)
                pe.wait_ge(y_added, NT * n + (l + 1))
                for m in range(4):
                    if m >= 2:
                        pe.wait_ge(silu_done, 4 * n + (m - 1))
                        pe.wait_ge(hid_done, 4 * n + (m - 1))
                    for w, first, done in ((W1, 4 * (m % 2), moe_g), (W3, 4 * (m % 2) + 2, moe_u)):
                        for k in range(KC):
                            for s in range(2):
                                last = nc.tensor.matmul(bank[:, first + s, 0:NTOK // 2],
                                                        weights(w[par])[:, k, P * m:P * m + P],
                                                        xT[:, k, NTOK // 2 * s:NTOK // 2 * (s + 1)],
                                                        start=(k == 0), stop=(k == KC - 1))
                        last.then_inc(done, 1)
                pe.wait_ge(w2_in[par], 16 * (pairs) + 16)
                pe.wait_ge(hid_done, 4 * n + 4)
                for t in range(NT):
                    if t == 4:
                        pe.wait_ge(y_added, NT * n + (l + 2))
                    for j in range(2):
                        for m in range(4):
                            last = nc.tensor.matmul(bank[0:ROWS[t], 2 * (t % 4) + j, :], hid[:, m, tok(t)],
                                                    weights(W2[par], 4)[:, m, 512 * j:512 * j + 512],
                                                    start=(m == 0), stop=(m == 3))
                    last.then_inc(moe_y, 1)

            attention("dsa")
            project_out(0, OUT_EVEN)
            turn_norm(1)
            router(0)
            experts(0)
            turn_norm(2)
            attention("sb")
            attention("diff")
            project_out(1, OUT_ODD)
            turn_norm(3)
            router(1)
            experts(1)

        @block.scalar
        def _(act):
            chain = [0]

            def link(ins):
                chain[0] += 1
                ins.then_inc(act_step, 1)
                act.wait_ge(act_step, chain[0])

            def copy_out(key, dst, src):
                return nc.scalar.copy(dst, src)

            def read(ins):
                ins.then_inc(bank_read["act"], 1)

            def norm(n):
                if n == 0:
                    act.wait_ge(zeros_set, 1)
                    act.wait_ge(x_in, 32)
                for t in range(NT):
                    if n in (1, 3):
                        taken(act, ("y", n // 2, t, 1))
                    if n in (2, 4) and t == 0:
                        act.wait_ge(y_added, (1 + NE * NT) * (n // 2))
                    if n in (1, 3) and t == 0:
                        pass
                    r = ROWS[t]
                    nc.scalar.activation(junk[0:r, :], h[0:r, t, :], ACT.Square,
                                         accum_out=ssq[0:r, n, t:t + 1]).then_inc(squared, 1)
                    act.wait_ge(squared, NT * n + t + 1)
                act.wait_ge(mean_ready, n + 1)
                nc.scalar.activation(std[:, n, :], mean[:, n, :], ACT.Sqrt).then_inc(std_ready, 1)

            def step_P(mech, t):
                r = ROWS[t]
                own = keys_at(t)[2]
                nf = 3 if mech == "dsa" else 4
                if t == NT - 1:
                    for b in range(2):
                        src = filled(act, (mech, "cache", b))[:, 0:P * nf].rearrange("p (f n) -> p f n", f=nf)
                        read(nc.scalar.copy(kT[:, 0:nf, SEQ + P * b:SEQ + P * b + P], src))
                if mech == "sb":
                    b = filled(act, (mech, "k", t))
                    if t > 0:
                        act.wait_ge(bank_filled, number[(mech, "kT", t - 1)] + 1)
                    act.wait_ge(out_rows, 16 * (2 * NT + t))
                    read(nc.scalar.copy(rows[0:r, 0:512], b[0:r, :]))
                if mech != "dsa":
                    b = filled(act, (mech, "v", t))
                    if t == 0:
                        act.wait_ge(out_vals, 16 * NT * (1 if mech == "sb" else 2))
                    read(nc.scalar.copy(vodd[0:r, own_block(t), :], b[0:r, :]))
                b = filled(act, (mech, "kT", t))
                read(nc.scalar.copy(kT[:, 0:nf, own:own + r],
                                    b[:, 0:P * nf].rearrange("p (f n) -> p f n", f=nf)[:, :, 0:r]))
                if mech == "dsa":
                    b = filled(act, (mech, "qiT", t))
                    read(nc.scalar.copy(qiT[:, t % 2, :, 0:r],
                                        b[:, 0:2 * P].rearrange("p (f n) -> p f n", f=2)[:, :, 0:r]))
                b = filled(act, (mech, "qT", t))
                read(nc.scalar.copy(qT[:, t % 2, :, 0:r],
                                    b[:, :].rearrange("p (f n) -> p f n", f=4)[:, :, 0:r]))
                if mech == "dsa":
                    nk = keys_at(t)[1]
                    for hd in range(4):
                        b = filled(act, (mech, "ix", t, hd))
                        if 4 * t + hd > 0:
                            act.wait_ge(index_ready, 4 * t + hd)
                        read(nc.scalar.activation(idxrel[0:r, 0:nk], b[0:r, 0:nk], ACT.Relu))

            def turned(mech, t, hd):
                r, blocks, n = ROWS[t], key_blocks(t), head_no(mech, t, hd)
                b = filled(act, (mech, "pT", t, hd))
                if n >= 2:
                    act.wait_ge(out_filled, n - 1)
                if t < 4:
                    nb = len(blocks)
                    read(nc.scalar.copy(probT[:, n % 2, 0:nb, 0:r],
                                        b[:, 0:P * nb].rearrange("p (b n) -> p b n", b=nb)))
                else:
                    nc.scalar.copy(probT[:, n % 2, 0:2, 0:r],
                                   b[:, 0:2 * P].rearrange("p (b n) -> p b n", b=2)[:, :, 0:r])
                    read(nc.scalar.copy(probT[0:DEC, n % 2, 2, 0:r], b[0:DEC, 2 * P:2 * P + r]))

            def step_A(mech, t):
                r, nk = ROWS[t], keys_at(t)[1]
                for step in range(HEADS[mech] + LAG[mech]):
                    hd = step
                    if hd < HEADS[mech]:
                        if mech == "dsa":
                            n = head_no(mech, t, hd)
                            taken(act, (mech, "s", t, hd, 0))
                            if n >= 2:
                                act.wait_ge(bank_filled, number[head_key(n - 2)] + 1)
                            if hd == 0 and tiles_before[mech] + t > 0:
                                act.wait_ge(out_read, tiles_before[mech] + t)
                            nc.scalar.activation(prob[0:r, n % 2, 0:nk], score[0:r, n % 2, 0:nk], ACT.Exp,
                                                 bias=least[0:r, hd, 0:1], scale=-1.0,
                                                 accum_out=rowsum[0:r, hd, 0:1]).then_inc(prob_ready, 1)
                        elif mech == "sb":
                            n = head_no(mech, t, hd)
                            taken(act, (mech, "s", t, hd, 0))
                            if n - heads_before["sb"] >= 2:
                                act.wait_ge(tail_ready, n - heads_before["sb"] - 1)
                            lp = logp[0:r, n % 2, 0:nk]
                            link(nc.scalar.activation(lp, score[0:r, n % 2, 0:nk], ACT.Abs))
                            link(nc.scalar.activation(lp, lp, ACT.Exp, scale=-1.0))
                            nc.scalar.activation(lp, lp, ACT.Ln, bias=1.0).then_inc(soft_ready, 1)
                        else:
                            for c in range(2):
                                n = map_no(mech, t, hd, c)
                                taken(act, (mech, "s", t, hd, c))
                                m = n - maps_before["diff"]
                                if m >= 4:
                                    act.wait_ge(prob_ready, head_no(mech, t, hd) - 1)
                                nc.scalar.activation(expo[0:r, n % 4, 0:nk], score[0:r, n % 2, 0:nk], ACT.Exp,
                                                     bias=least[0:r, n % 8, 0:1], scale=-1.0,
                                                     accum_out=rowsum[0:r, n % 8, 0:1]).then_inc(exp_done, 1)
                    hd = step - 1
                    if mech == "sb" and 0 <= hd < HEADS[mech]:
                        n = head_no(mech, t, hd)
                        act.wait_ge(expo_in, n - heads_before["sb"] + 1)
                        pr = prob[0:r, n % 2, 0:nk]
                        nc.scalar.activation(pr, pr, ACT.Exp).then_inc(prob_ready, 1)
                    hd = step - LAG[mech]
                    if mech != "sb" and 0 <= hd < HEADS[mech]:
                        turned(mech, t, hd)
                if mech == "diff":
                    act.wait_ge(osq_ready, t + 1)
                    link(nc.scalar.activation(oln[0:r, :], oms[0:r, :], ACT.Ln))
                    nc.scalar.activation(ors[0:r, :], oln[0:r, :], ACT.Exp, scale=-0.5).then_inc(ors_ready, 1)

            heads = [(m, t, hd) for m in MECHS for t in range(NT) for hd in range(HEADS[m])]

            def head_key(n):
                m, t, hd = heads[n]
                return (m, "pT", t, hd)

            def step_O(mech, t):
                r = ROWS[t]
                src = filled(act, (mech, "oT", t))[:, :].rearrange("p (f n) -> p f n", f=4)[:, :, 0:r]
                f = 0 if mech == "sb" else 4
                if mech == "diff":
                    if t == 0:
                        act.wait_ge(lam_exps, 2)
                    read(nc.scalar.activation(mixT[:, f:f + 4, tok(t)], src, ACT.Copy, scale=gain_out))
                else:
                    read(nc.scalar.copy(mixT[:, f:f + 4, tok(t)], src))

            def step_U(g):
                for key, lo_, hi_ in ((("dsa", "a", g), 0, SEQ), (("dsa", "as", g), SEQ, NTOK)):
                    b = filled(act, key)
                    read(nc.scalar.activation(mixT[:, g, lo_:hi_], b[:, 0:hi_ - lo_], ACT.Copy,
                                              scale=scale_pool[:, g:g + 1]))

            def attention(mech):
                for kind, t in schedule(mech):
                    if kind == "P":
                        step_P(mech, t)
                    elif kind == "A":
                        step_A(mech, t)
                    elif kind == "O":
                        step_O(mech, t)
                    else:
                        step_U(t)

            def router(l):
                act.wait_ge(route_in, l + 1)
                nc.scalar.activation(r_exp, r_arg, ACT.Exp).then_inc(route_exp, 1)

            def experts(l):
                with act.Fori(0, NE // 2) as i:
                    for par in range(2):
                        n = 2 * i + (l * NE + par)
                        for m in range(4):
                            act.wait_ge(moe_g, 4 * n + (m + 1))
                            if m >= 2:
                                act.wait_ge(hid_done, 4 * n + (m - 1))
                            nc.scalar.activation(silu[:, m % 2, :, :],
                                                 bank[:, 4 * (m % 2):4 * (m % 2) + 2, 0:NTOK // 2],
                                                 ACT.Silu).then_inc(silu_done, 1)

            norm(0)
            for f in range(4):
                b = filled(act, ("u", f))
                read(nc.scalar.copy(uT[:, f, HIST:HIST + SEQ], b))
            b = filled(act, ("us",))
            read(nc.scalar.copy(uT[:, :, USAM:UEXT], b[:, 0:4 * DEC].rearrange("p (f n) -> p f n", f=4)))
            b = filled(act, ("hist",))
            read(nc.scalar.copy(uT[:, :, HIST + SEQ:USAM],
                                b[:, 0:64].rearrange("p (f n) -> p f n", f=4)[:, :, 0:HIST]))
            for i, (key, dst) in enumerate(((("pool_p",), pool_p), (("pool_s",), pool_s))):
                b = filled(act, key)
                link_dst = (poolout, histrow)[i][0:HIST, :]
                chain[0] += 1
                read(nc.scalar.copy(link_dst, b[0:HIST, :]))
                act.wait_ge(bank_read["act"], rank[key])
                act.dma_start(dst[0, 0], link_dst).then_inc(out_pool, 16)
                chain[0] -= 1
            attention("dsa")
            norm(1)
            router(0)
            experts(0)
            act.wait_ge(lam_dots, 1)
            nc.scalar.activation(lam_exp, lam_dot, ACT.Exp).then_inc(lam_exps, 1)
            norm(2)
            attention("sb")
            attention("diff")
            norm(3)
            router(1)
            experts(1)
            norm(4)

        @block.vector
        def _(dve):
            chain = [0]
            tt = nc.vector.tensor_tensor

            def link(ins):
                chain[0] += 1
                ins.then_inc(dve_step, 1)
                dve.wait_ge(dve_step, chain[0])

            def read(ins, key):
                ins.then_inc(bank_read["dve"], 1)
                dve.wait_ge(bank_read["dve"], rank[key])

            link(nc.vector.memset(stats[:, :], 1.0))
            link(nc.vector.memset(logits, 0.0))
            nc.vector.memset(uT[:, :, 0:HIST], 0.0).then_inc(zeros_set, 1)

            def norm(n):
                dve.wait_ge(squared, NT * (n + 1))
                nc.vector.tensor_scalar(mean[:, n, :], ssq[:, n, :], 1.0 / DM, EPS, ALU.mult, ALU.add)\
                  .then_inc(mean_ready, 1)
                dve.wait_ge(std_ready, n + 1)
                link(nc.vector.reciprocal(rstd[:, n, :], std[:, n, :]))
                for t in range(NT):
                    r = ROWS[t]
                    if n < 4:
                        nc.vector.tensor_scalar(xn[0:r, t, :], h[0:r, t, :], rstd[0:r, n, t:t + 1], None,
                                                ALU.mult).then_inc(xn_ready, 1)
                    else:
                        if t == 0:
                            dve.wait_ge(gfin_in, 16)
                        nc.vector.scalar_tensor_tensor(out=fin[0:r, t, :], in0=h[0:r, t, :],
                                                       scalar=rstd[0:r, n, t:t + 1], in1=gfin[0:r, :],
                                                       op0=ALU.mult, op1=ALU.mult).then_inc(fin_ready, 1)
                if n == 4:
                    return
                for t in range(NT):
                    r = ROWS[t]
                    for j in range(2):
                        key = ("xT", n, t, j)
                        b = filled(dve, key)[:, :].rearrange("p (k n) -> p k n", k=4)[:, :, 0:r]
                        g = g_norm[:, n, 4 * j:4 * j + 4].unsqueeze(2).broadcast_to([P, 4, r])
                        read(tt(xT[:, 4 * j:4 * j + 4, tok(t)], b, g, ALU.mult), key)

            def rope_products(bank_ap, t, c, n, at_):
                r = ROWS[t]
                hd = n // HD
                x4 = bank_ap[0:r, c:c + n].rearrange("p (h s e) -> p h s e", s=2, e=32)
                for table, dst in ((cos, ropeA), (sin, ropeB)):
                    tab = table[0:r, t, :].unsqueeze(1).unsqueeze(1).broadcast_to([r, hd, 2, 32])
                    last = tt(dst[0:r, at_:at_ + n].rearrange("p (h s e) -> p h s e", s=2, e=32), x4, tab,
                              ALU.mult)
                return last

            def rope_free(mech, t, part):
                n = rope_no(mech, t, part)
                if n > 0:
                    dve.wait_ge(rope_out, n)

            def step_P(mech, t):
                r = ROWS[t]
                if mech == "dsa":
                    key = (mech, "kv", t)
                    b = filled(dve, key)
                    if t == 0:
                        dve.wait_ge(out_pool, 32)
                    rope_free(mech, t, 0)
                    rope_products(b, t, 0, 128, 0)
                    rope_products(b, t, 256, 256, 128)
                    read(nc.vector.tensor_copy(vdsa[0:r, own_block(t), :], b[0:r, 128:256]), key)
                    key = (mech, "ki", t)
                    b = filled(dve, key)
                    rope_products(b, t, 0, 64, 384)
                    read(nc.vector.tensor_scalar(w_idx[0:r, t % 2, :], b[0:r, 64:68], 0.0625, None,
                                                 ALU.mult), key)
                    key = (mech, "q", t)
                    b = filled(dve, key)
                    rope_free(mech, t, 1)
                    read(rope_products(b, t, 0, 512, 0), key)
                    index(t)
                    return
                if mech == "diff":
                    for part, name in enumerate("kq"):
                        key = (mech, name, t)
                        b = filled(dve, key)
                        rope_free(mech, t, part)
                        read(rope_products(b, t, 0, 512, 0), key)
                else:
                    key = (mech, "q", t)
                    b = filled(dve, key)
                    if t > 0:
                        dve.wait_ge(bank_filled, number[(mech, "qT", t - 1)] + 1)
                    else:
                        dve.wait_ge(out_rows, 16 * 2 * NT)
                    read(nc.vector.tensor_copy(rows[0:r, 512:1024], b[0:r, :]), key)

            def index(t):
                r, nk = ROWS[t], keys_at(t)[1]
                acc = idxacc[0:r, 0:nk]
                adm = const[0:r, C_CHUNK + 512 - nk:C_CHUNK + 512] if t < 4 else \
                    const[0:r, C_CHUNK + 128:C_CHUNK + 128 + nk]
                for hd in range(4):
                    taken(dve, ("dsa", "ix", t, hd))
                    nc.vector.scalar_tensor_tensor(out=acc, in0=idxrel[0:r, 0:nk],
                                                   scalar=w_idx[0:r, t % 2, hd:hd + 1],
                                                   in1=adm if hd == 0 else acc, op0=ALU.mult, op1=ALU.add)\
                      .then_inc(index_ready, 1)
                    dve.wait_ge(index_ready, 4 * t + hd + 1)
                if t == 0:
                    link(nc.vector.tensor_copy(selected[0:r, 0, 0:nk], adm))

            def select_rounds(t, lo_, hi_):
                r, nk = ROWS[t], keys_at(t)[1]
                total = (PROMPT_SEL if t < 4 else SAMPLE_SEL) // 8
                acc = idxacc[0:r, 0:nk]
                for i in range(lo_, min(hi_, total)):
                    link(nc.vector.max(top8[0:r, :], acc))
                    link(nc.vector.match_replace(acc, top8[0:r, :], acc, TAKEN))
                    if i == total - 1:
                        link(nc.vector.tensor_scalar(selected[0:r, t % 2, 0:nk], acc, 2.0 * NEG, NEG,
                                                     ALU.is_ge, ALU.mult))

            def step_A(mech, t):
                r, nk = ROWS[t], keys_at(t)[1]
                k0 = keys_at(t)[0]
                tile = tiles_before[mech] + t
                causal = {"dsa": None, "sb": C_CAUSAL, "diff": C_CHUNK}[mech]
                if causal is None:
                    mask = selected[0:r, t % 2, 0:nk]
                elif t < 4:
                    mask = const[0:r, causal + 512 - nk:causal + 512]
                else:
                    mask = const[0:r, causal + 128:causal + 128 + nk]
                for step in range(HEADS[mech] + LAG[mech]):
                    hd = step
                    if hd < HEADS[mech]:
                        for c in range(2 if mech == "diff" else 1):
                            key = (mech, "s", t, hd, c)
                            b = filled(dve, key)
                            n = map_no(mech, t, hd, c)
                            m = n - maps_before[mech]
                            sc = score[0:r, n % 2, 0:nk]
                            if mech == "sb":
                                if m >= 2:
                                    dve.wait_ge(expo_in, m - 1)
                                read(nc.vector.scalar_tensor_tensor(out=sc, in0=b[0:r, 0:nk], scalar=0.125,
                                                                    in1=mask, op0=ALU.mult, op1=ALU.add), key)
                            else:
                                if m >= 2:
                                    if mech == "dsa":
                                        dve.wait_ge(prob_ready, n - 1)
                                    else:
                                        dve.wait_ge(exp_done, m - 1)
                                lcol = hd if mech == "dsa" else n % 8
                                read(nc.vector.tensor_tensor_reduce(sc, b[0:r, 0:nk], mask, -0.125, 3e38,
                                                                    ALU.add, ALU.min,
                                                                    least[0:r, lcol, 0:1]), key)
                        if mech == "dsa" and t + 1 < NT:
                            select_rounds(t + 1, 2 * hd, 2 * hd + 2)
                    hd = step - 1
                    if mech == "sb" and 0 <= hd < HEADS[mech]:
                        n = head_no(mech, t, hd)
                        m = n - heads_before["sb"]
                        dve.wait_ge(soft_ready, m + 1)
                        lp, sc, tl = (x[0:r, n % 2, 0:nk] for x in (logp, score, tail))
                        link(nc.vector.scalar_tensor_tensor(out=lp, in0=sc, scalar=0.0, in1=lp, op0=ALU.max,
                                                            op1=ALU.add))
                        if m >= 2:
                            dve.wait_ge(expo_in, m - 1)
                        nc.vector.tensor_tensor_scan(tl[:, ::-1], lp[:, ::-1], lp[:, ::-1], 0.0, ALU.add,
                                                     ALU.bypass).then_inc(tail_ready, 1)
                    if mech == "diff" and 0 <= hd < HEADS[mech]:
                        n = head_no(mech, t, hd)
                        m0 = map_no(mech, t, hd, 0)
                        dve.wait_ge(exp_done, m0 - maps_before["diff"] + 2)
                        c0 = m0 % 8
                        link(nc.vector.reciprocal(rinv[0:r, c0:c0 + 2, 0], rowsum[0:r, c0:c0 + 2, 0]))
                        link(nc.vector.tensor_scalar(rinv[0:r, c0 + 1, 1:2], rinv[0:r, c0 + 1, 0:1],
                                                     lam[0:r, :], None, ALU.mult))
                        e1 = expo[0:r, (m0 + 1) % 4, 0:nk]
                        link(nc.vector.tensor_scalar(e1, e1, rinv[0:r, c0 + 1, 1:2], None, ALU.mult))
                        if n >= heads_before["diff"] + 2:
                            dve.wait_ge(bank_filled, number[(mech, "pT") + divmod(n - 2 - heads_before["diff"], 4)]
                                        + 1)
                        nc.vector.scalar_tensor_tensor(out=prob[0:r, n % 2, 0:nk],
                                                       in0=expo[0:r, m0 % 4, 0:nk],
                                                       scalar=rinv[0:r, c0, 0:1], in1=e1, op0=ALU.mult,
                                                       op1=ALU.subtract).then_inc(prob_ready, 1)
                    hd = step - LAG[mech]
                    if mech == "sb" and 0 <= hd < HEADS[mech]:
                        turned(mech, t, hd)
                dve.wait_ge(out_filled, head_no(mech, t, HEADS[mech] - 1) + 1)
                out = bank[0:r, NB + tile % 2, :]
                o = orow[0:r, tile % 2, :]
                if tile >= 2:
                    m2, t2 = MECHS[(tile - 2) // NT], (tile - 2) % NT
                    dve.wait_ge(bank_filled, number[(m2, "oT", t2)] + 1)
                if mech == "dsa":
                    link(nc.vector.reciprocal(rinv[0:r, :, 0], rowsum[0:r, :, 0]))
                    tt(o.rearrange("p (h d) -> p h d", h=8), out.rearrange("p (h d) -> p h d", h=8),
                       rinv[0:r, :, 0:1].broadcast_to([r, 8, HD]), ALU.mult).then_inc(out_read, 1)
                elif mech == "sb":
                    nc.vector.tensor_copy(o, out).then_inc(out_read, 1)
                else:
                    link(nc.vector.tensor_copy(o, out))
                    for hd in range(4):
                        sl = slice(P * hd, P * hd + P)
                        link(nc.vector.tensor_tensor_reduce(odd_junk[0:r, sl], o[:, sl], o[:, sl], 1.0, 0.0,
                                                            ALU.mult, ALU.add, osq[0:r, hd:hd + 1]))
                    nc.vector.tensor_scalar(oms[0:r, :], osq[0:r, :], 1.0 / P, EPS, ALU.mult, ALU.add)\
                      .then_inc(osq_ready, 1)
                    dve.wait_ge(ors_ready, t + 1)
                    o3 = o.rearrange("p (h d) -> p h d", h=4)
                    tt(o3, o3, ors[0:r, :].unsqueeze(2).broadcast_to([r, 4, P]), ALU.mult)\
                      .then_inc(out_read, 1)

            def turned(mech, t, hd):
                r, blocks, n = ROWS[t], key_blocks(t), head_no(mech, t, hd)
                key = (mech, "pT", t, hd)
                b = filled(dve, key)
                dve.wait_ge(out_filled, n - 1)
                if t < 4:
                    nb = len(blocks)
                    read(nc.vector.tensor_copy(probT[:, n % 2, 0:nb, 0:r],
                                               b[:, 0:P * nb].rearrange("p (b n) -> p b n", b=nb)), key)
                else:
                    nc.vector.tensor_copy(probT[:, n % 2, 0:2, 0:r],
                                          b[:, 0:2 * P].rearrange("p (b n) -> p b n", b=2)[:, :, 0:r])
                    read(nc.vector.tensor_copy(probT[0:DEC, n % 2, 2, 0:r], b[0:DEC, 2 * P:2 * P + r]), key)

            def step_U(g):
                w = WINDOWS[g]
                dve.wait_ge(sums_ready, g + 1)
                s = (sumA, sumB)[g % 2]
                if g > 0:
                    dve.wait_ge(bank_filled, number[("dsa", "as", g - 1)] + 1)
                link(nc.vector.scalar_tensor_tensor(out=pooled, in0=s[:, HIST:HIST + SEQ],
                                                    scalar=1.0 / w, in1=uT[:, g, HIST:HIST + SEQ],
                                                    op0=ALU.mult, op1=ALU.subtract))
                link(nc.vector.scalar_tensor_tensor(out=pooled_s, in0=s[:, USAM:UEXT],
                                                    scalar=1.0 / w, in1=uT[:, g, USAM:UEXT],
                                                    op0=ALU.mult, op1=ALU.subtract))
                head = pooled[:, 0:16]
                link(tt(head, s[:, HIST:HIST + 16], const[:, C_RCNT + 16 * g:C_RCNT + 16 * g + 16], ALU.mult))
                tt(head, head, uT[:, g, HIST:HIST + 16], ALU.subtract).then_inc(pooled_ready, 1)

            def attention(mech):
                for kind, t in schedule(mech):
                    if kind == "P":
                        step_P(mech, t)
                    elif kind == "A":
                        step_A(mech, t)
                    elif kind == "U":
                        step_U(t)

            def add_out(layer):
                for t in range(NT):
                    for j in range(2):
                        key = ("y", layer, t, j)
                        b = filled(dve, key)
                        hh = h[0:ROWS[t], t, 512 * j:512 * j + 512]
                        read(tt(hh, b[0:ROWS[t], :], hh, ALU.add), key)

            def router(l):
                key = ("router", l)
                b = filled(dve, key)
                tt(logits[:, 0:4, :], b[:, 0:80].rearrange("p (t n) -> p t n", t=4),
                   b_router[:, l, :].unsqueeze(1).broadcast_to([P, 4, 20]), ALU.add)
                read(tt(logits[0:DEC, 4, :], b[0:DEC, 80:100], b_router[0:DEC, l, :], ALU.add), key)

                def part(a, n):
                    return route[:, a:a + n * NT].rearrange("p (t n) -> p t n", t=NT)

                js = const[:, C_J:C_J + 4].unsqueeze(1).broadcast_to([P, NT, 4])
                gmax, v1, v2, low = part(50, 1), part(55, 1), part(60, 1), part(65, 1)
                g_hot, hot1, hot2, eq, e_sel = (part(70 + 20 * i, 4) for i in range(5))
                e_all = part(170, 16)
                w_1, w_2, gs = part(250, 1), part(255, 1), part(260, 1)
                x_exp, g_exp = r_exp[:, 0:5].unsqueeze(2), r_exp[:, 5:25].rearrange("p (t n) -> p t n", t=NT)
                x_arg, g_arg = r_arg[:, 0:5].unsqueeze(2), r_arg[:, 5:25].rearrange("p (t n) -> p t n", t=NT)

                def bc(x, n=4):
                    return x.broadcast_to([P, NT, n])

                def first_max(src, top, hot):
                    link(nc.vector.tensor_reduce(top[:, :, 0], src, AX_X, ALU.max))
                    link(tt(eq, src, bc(top), ALU.is_equal))
                    link(nc.vector.scalar_tensor_tensor(out=eq, in0=eq, scalar=-8.0, in1=js, op0=ALU.mult,
                                                        op1=ALU.add))
                    link(nc.vector.tensor_reduce(low[:, :, 0], eq, AX_X, ALU.min))
                    link(tt(hot, eq, bc(low), ALU.is_equal))

                lg, le = logits[:, :, 0:4], logits[:, :, 4:20]
                first_max(lg, gmax, g_hot)
                link(tt(g_arg, lg, bc(gmax), ALU.subtract))
                le4 = le.rearrange("p t (g j) -> p t g j", g=4)
                ea4 = e_all.rearrange("p t (g j) -> p t g j", g=4)
                link(tt(ea4, le4, g_hot.unsqueeze(3).broadcast_to([P, NT, 4, 4]), ALU.mult))
                link(nc.vector.tensor_reduce(e_sel, ea4.rearrange("p t g j -> p t j g"), AX_X, ALU.add))
                first_max(e_sel, v1, hot1)
                link(nc.vector.scalar_tensor_tensor(out=e_sel, in0=hot1, scalar=-3e38, in1=e_sel,
                                                    op0=ALU.mult, op1=ALU.add))
                first_max(e_sel, v2, hot2)
                tt(x_arg, v2, v1, ALU.subtract).then_inc(route_in, 1)
                dve.wait_ge(route_exp, l + 1)
                link(nc.vector.tensor_reduce(gs[:, :, 0], g_exp, AX_X, ALU.add))
                link(nc.vector.scalar_tensor_tensor(out=w_2, in0=x_exp, scalar=1.0, in1=gs, op0=ALU.add,
                                                    op1=ALU.mult))
                link(nc.vector.reciprocal(w_1, w_2))
                link(tt(w_2, w_1, x_exp, ALU.mult))
                link(tt(hot1, hot1, bc(w_1), ALU.mult))
                link(tt(hot2, hot2, bc(w_2), ALU.mult))
                link(tt(hot1, hot1, hot2, ALU.add))
                g4 = gate.rearrange("p t (g j) -> p t g j", g=4)
                tt(g4, g_hot.unsqueeze(3).broadcast_to([P, NT, 4, 4]),
                   hot1.unsqueeze(2).broadcast_to([P, NT, 4, 4]), ALU.mult).then_inc(y_added, 1)
                dve.wait_ge(y_added, (1 + NE * NT) * l + 1)

            def experts(l):
                with dve.Fori(0, NE // 2) as i:
                    for par in range(2):
                        n = 2 * i + (l * NE + par)
                        for m in range(4):
                            dve.wait_ge(silu_done, 4 * n + (m + 1))
                            dve.wait_ge(moe_u, 4 * n + (m + 1))
                            tt(hid[:, m, :].rearrange("p (s n) -> p s n", s=2), silu[:, m % 2, :, :],
                               bank[:, 4 * (m % 2) + 2:4 * (m % 2) + 4, 0:NTOK // 2], ALU.mult)\
                              .then_inc(hid_done, 1)
                        for t in range(NT):
                            r = ROWS[t]
                            dve.wait_ge(moe_y, NT * n + (t + 1))
                            hh = h[0:r, t, :].rearrange("p (j n) -> p j n", j=2)
                            nc.vector.scalar_tensor_tensor(
                                out=hh, in0=bank[0:r, 2 * (t % 4):2 * (t % 4) + 2, :],
                                scalar=gate[0:r, t, bass.ds(2 * i + par, 1)], in1=hh, op0=ALU.mult,
                                op1=ALU.add).then_inc(y_added, 1)
                        dve.wait_ge(y_added, NT * n + (NT + l + 1))

            dve.wait_ge(const_in, 16)
            dve.wait_ge(small_in, 16 * SMALL_LOADS)
            dots = lam_in.rearrange("p (a n) -> p a n", a=4)
            for i in range(2):
                link(nc.vector.tensor_tensor_reduce(lam_tmp, dots[:, 2 * i, :], dots[:, 2 * i + 1, :], 1.0, 0.0,
                                                    ALU.mult, ALU.add, lam_dot[:, i:i + 1]))
            nc.vector.tensor_scalar(gain_out, gain_diff, 1.0 - LAM_INIT, None, ALU.mult).then_inc(lam_dots, 1)
            norm(0)
            attention("dsa")
            add_out(0)
            norm(1)
            router(0)
            experts(0)
            dve.wait_ge(lam_exps, 1)
            link(tt(lam, lam_exp[:, 0:1], lam_exp[:, 1:2], ALU.subtract))
            nc.vector.tensor_scalar(lam, lam, LAM_INIT, None, ALU.add).then_inc(lam_exps, 1)
            dve.wait_ge(lam_exps, 2)
            norm(2)
            attention("sb")
            attention("diff")
            add_out(1)
            norm(3)
            router(1)
            experts(1)
            norm(4)

        @block.gpsimd
        def _(pool):
            chain = [0]

            def link(ins):
                chain[0] += 1
                ins.then_inc(pool_step, 1)
                pool.wait_ge(pool_step, chain[0])

            gtt = nc.gpsimd.tensor_tensor

            def rotate(dst, src_at, n, t, dup=False):
                r = ROWS[t]
                hd = n // HD
                a, b = (x[0:r, src_at:src_at + n].rearrange("p (h s e) -> p h s e", s=2, e=32)
                        for x in (ropeA, ropeB))
                for s, op in ((0, ALU.subtract), (1, ALU.add)):
                    x, y = a[:, :, s, :], b[:, :, 1 - s, :]
                    if dup:
                        d = dst.rearrange("p (h u s e) -> p h u s e", u=2, s=2, e=32)[:, :, :, s, :]
                        x, y = (z.unsqueeze(2).broadcast_to([r, hd, 2, 32]) for z in (x, y))
                    else:
                        d = dst.rearrange("p (h s e) -> p h s e", s=2, e=32)[:, :, s, :]
                    last = gtt(d, x, y, op)
                return last

            def store_rows(mech, t):
                r = ROWS[t]
                sl = slice(P * t, P * t + P) if t < 4 else slice(0, DEC)
                if mech == "dsa":
                    kd, vd, kid = (dsak_p, dsav_p, idxk_p) if t < 4 else (dsak_s, dsav_s, idxk_s)
                    src = rows[0:r, 0:256].rearrange("p (g u d) -> p g u d", g=2, u=2)[:, :, 0, :]
                    pool.dma_start(kd[0, 0, sl], src).then_inc(out_rows, 16)
                    pool.dma_start(kid[0, 0, sl], rows[0:r, 512:576]).then_inc(out_rows, 16)
                    taken(pool, (mech, "kv", t))
                    pool.dma_start(rows2d(vd)[sl, :], vdsa[0:r, own_block(t), :]).then_inc(out_vals, 16)
                    return
                kd, vd = {"sb": ((sbk_p, sbv_p), (sbk_s, sbv_s)), "diff": ((dfk_p, dfv_p), (dfk_s, dfv_s))}[mech][t // 4]
                kd = kd if mech == "sb" else kd.rearrange("a b s g c d -> a b s (g c) d")
                pool.dma_start(rows2d(kd)[sl, :], rows[0:r, 0:512]).then_inc(out_rows, 16)
                taken(pool, (mech, "v", t))
                pool.dma_start(rows2d(vd)[sl, :], vodd[0:r, own_block(t), :]).then_inc(out_vals, 16)

            def step_P(mech, t):
                r = ROWS[t]
                if mech == "sb":
                    taken(pool, (mech, "k", t))
                    store_rows(mech, t)
                    return
                if t > 0:
                    pool.wait_ge(bank_filled, number[(mech, "qT", t - 1)] + 1)
                elif mech == "diff":
                    pool.wait_ge(bank_filled, number[("sb", "qT", NT - 1)] + 1)
                done = {"dsa": 2 * t, "diff": 3 * NT + t}[mech]
                if done:
                    pool.wait_ge(out_rows, 16 * done)
                taken(pool, (mech, "ki" if mech == "dsa" else "k", t))
                if mech == "dsa":
                    rotate(rows[0:r, 0:256], 0, 128, t, dup=True)
                    rotate(rows[0:r, 256:512], 128, 256, t)
                    rotate(rows[0:r, 512:640], 384, 64, t, dup=True).then_inc(rope_out, 1)
                else:
                    rotate(rows[0:r, 0:512], 0, 512, t).then_inc(rope_out, 1)
                taken(pool, (mech, "q", t))
                q_at = 640 if mech == "dsa" else 512
                rotate(rows[0:r, q_at:q_at + 512], 0, 512, t).then_inc(rope_out, 1)
                pool.wait_ge(rope_out, rope_no(mech, t, 1) + 1)
                store_rows(mech, t)

            def step_A(mech, t):
                if mech != "sb":
                    return
                r, nk = ROWS[t], keys_at(t)[1]
                for hd in range(8):
                    n = head_no(mech, t, hd)
                    m = n - heads_before["sb"]
                    pool.wait_ge(tail_ready, m + 1)
                    if m >= 2:
                        t2, h2 = divmod(m - 2, 8)
                        pool.wait_ge(bank_filled, number[("sb", "pT", t2, h2)] + 1)
                    gtt(prob[0:r, n % 2, 0:nk], score[0:r, n % 2, 0:nk], tail[0:r, n % 2, 0:nk],
                        ALU.subtract).then_inc(expo_in, 1)

            def sums(g):
                if g == 0:
                    taken(pool, ("hist",))
                    pool.wait_ge(zeros_set, 1)
                src, width = uT[:, g, :], 1
                if g >= 2:
                    pool.wait_ge(pooled_ready, g - 1)
                for i in range(g + 1):
                    dst = (sumA, sumB)[(g - i + g) % 2] if False else (sumA, sumB)[(g + (g - i)) % 2]
                    first = 2 * width - 1
                    if g >= 1:
                        pool.wait_ge(pooled_ready, g)
                    ins = gtt(dst[:, first:UEXT], src[:, first:UEXT], src[:, first - width:UEXT - width], ALU.add)
                    if i == g:
                        ins.then_inc(sums_ready, 1)
                    else:
                        link(ins)
                    src, width = dst, 2 * width

            for mech in MECHS:
                for kind, t in schedule(mech):
                    if kind == "P":
                        step_P(mech, t)
                    elif kind == "A":
                        step_A(mech, t)
                    elif kind == "U":
                        sums(t)


SMALL_LOADS = 4 + 2 + 2 * 5 + 2 * 2 + 1

_INS = ['x_prompt', 'x_sample', 'cache_pool', 'cache_dsa_k', 'cache_dsa_v', 'cache_idx_k', 'cache_sb_k',
        'cache_sb_v', 'cache_diff_k', 'cache_diff_v', 'norm_mix', 'norm_ffn', 'norm_final', 'w_in_even',
        'w_pool', 'pool_scale', 'w_out_even', 'w_in_odd', 'diff_lambda', 'diff_subln', 'w_out_odd',
        'moe_w_group', 'moe_b_group', 'moe_w_expert', 'moe_b_expert', 'moe_w1', 'moe_w3', 'moe_w2']
_OUTS = [(1, 512, 1024), (1, 32, 1024),
         (1, 1, 15, 512), (1, 1, 512, 2, 64), (1, 1, 512, 2, 64), (1, 1, 512, 64),
         (1, 1, 512, 8, 64), (1, 1, 512, 8, 64), (1, 1, 512, 4, 2, 64), (1, 1, 512, 4, 128),
         (1, 1, 15, 512), (1, 1, 32, 2, 64), (1, 1, 32, 2, 64), (1, 1, 32, 64),
         (1, 1, 32, 8, 64), (1, 1, 32, 8, 64), (1, 1, 32, 4, 2, 64), (1, 1, 32, 4, 128)]


def _constants():
    import numpy as np
    c = np.zeros((P, C_N), np.float32)
    half = HD // 2
    inv = (np.float32(10000.0) ** (-np.arange(half, dtype=np.float32) / np.float32(half))).astype(np.float32)
    p = np.arange(P)
    for t in range(NT):
        pos = (P * t if t < 4 else PAST) + p
        ang = pos.astype(np.float32)[:, None] * inv[None, :]
        c[:, C_COS + 32 * t:C_COS + 32 * t + 32] = np.cos(ang)
        c[:, C_SIN + 32 * t:C_SIN + 32 * t + 32] = np.sin(ang)
    c[:, C_ID:C_ID + P] = np.eye(P)
    k = np.arange(P)
    c[:, C_CHUNK + 384:C_CHUNK + 512] = np.where(k[None, :] < (p[:, None] // CHUNK + 1) * CHUNK, 0.0, NEG)
    c[:, C_CAUSAL + 384:C_CAUSAL + 512] = np.where(k[None, :] < p[:, None], 0.0, NEG)
    for g, w in enumerate(WINDOWS):
        c[:, C_RCNT + 16 * g:C_RCNT + 16 * g + 16] = 1.0 / np.minimum(np.arange(16) + 1, w)
    c[:, C_J:C_J + 4] = np.arange(4)
    return c


def kernel(**inputs):
    import numpy as _np
    import concourse.bacc as _bacc
    from concourse import mybir as _mybir
    from concourse.bass_utils import run_bass_kernel_spmd as _run

    nc = _bacc.Bacc("TRN2", target_bir_lowering=False, num_devices=1)
    arrays, args = {}, []
    for name in _INS:
        arrays[f"in_{name}"] = _np.ascontiguousarray(inputs[name])
    arrays["in_constants"] = _constants()
    for name, a in arrays.items():
        args.append(nc.dram_tensor(name, a.shape, _mybir.dt.from_np(a.dtype), kind="ExternalInput").ap())
    for i, shape in enumerate(_OUTS):
        args.append(nc.dram_tensor(f"out_{i}", shape, _mybir.dt.float32, kind="ExternalOutput").ap())
    stream_kernel(nc, *args)
    r = _run(nc, [arrays], core_ids=[0])
    return tuple(r.results[0][f"out_{i}"] for i in range(len(_OUTS)))
```

```python
import concourse.bass as bass
from concourse import mybir
from contextlib import ExitStack

F32 = mybir.dt.float32
U32 = mybir.dt.uint32
I32 = mybir.dt.int32
ALU = mybir.AluOpType
ACT = mybir.ActivationFunctionType
AX_X = mybir.AxisListType.X

P = 128
DM = 1024
KC = DM // P
SEQ, DEC, PAST = 512, 32, 256
NT = 5
ROWS = [P] * 4 + [DEC]
NTOK = SEQ + DEC
NKEY = SEQ + PAST + DEC
HD = 64
CHUNK = 64
HIST = 15
WINDOWS = (2, 4, 8, 16)
UEXT = HIST + SEQ + HIST + DEC
USAM = HIST + SEQ + HIST
PROMPT_SEL, SAMPLE_SEL = 128, 72
KIW = 68
NE = 16
FH = 512
CAP = 96
EPS = 1e-6
NEG = -1e30
TAKEN = -3e38
LAM_INIT = 0.8 - 0.6 * 0.7408182206817179

C_COS, C_SIN, C_ID, C_CHUNK, C_CAUSAL, C_RCNT, C_IOTA, C_TOKEN, C_EPS = 0, 160, 320, 448, 960, 1472, 1536, 1632, 1637
C_N = 1638

S_U, S_Q, S_KV = 0, 1, 2
SB_K, SB_V, SB_Q = 1, 2, 0
DF_K, DF_V, DF_Q = 4, 1, 2
OUT_EVEN, OUT_ODD = (0, 4), (0, 4)
W1, W3, W2 = (1, 3), (2, 5), (0, 4)


def tok(t):
    return slice(P * t, P * t + ROWS[t])


def keys_at(t):
    return (0, P * (t + 1), P * t) if t < 4 else (SEQ, PAST + DEC, SEQ + PAST)


def key_blocks(t):
    return [(b, P) for b in range(t + 1)] if t < 4 else [(4, P), (5, P), (6, DEC)]


def own_block(t):
    return t if t < 4 else 6


HEADS = {"dsa": 8, "sb": 8, "diff": 4}
LN_EXP_SET = 6
LAG = {"dsa": 2, "sb": 3, "diff": 2}
ITEMS = {"dsa": ("kv", "ki", "q", "kT", "qiT", "qT", "ix0", "ix1", "ix2", "ix3"),
         "sb": ("k", "v", "q", "kT", "qT"), "diff": ("k", "v", "q", "kT", "qT")}


def schedule():
    out = []

    def stream(mech, extra):
        heads = HEADS[mech]
        for g in range(NT * heads + LAG[mech] + 1):
            out.append(("A", mech, g))
            last = g - LAG[mech] - 1
            if last >= 0 and last % heads == heads - 1:
                out.append(("F", mech, last // heads))
            out.extend(extra.get(divmod(g, heads), ()))

    def project(mech, t, *items):
        return [("P", mech, t, i) for i in items]

    def merged(into, more):
        for k, v in more.items():
            into.setdefault(k, []).extend(v)

    def last_rows(layer, mech):
        n = 2 * layer + 1
        return [("y", layer, 3, 1), ("O", mech, 4), ("N", n, 3), ("X", n, 3), ("y", layer, 4, 0),
                ("y", layer, 4, 1), ("T", n, 3), ("N", n, 4), ("X", n, 4), ("T", n, 4), ("router", layer),
                ("experts", layer)]

    for t in range(NT + 2):
        if t < NT:
            out.append(("N", 0, t))
        if 1 <= t <= NT:
            out.append(("X", 0, t - 1))
        if t >= 2:
            out.append(("T", 0, t - 2))
    out.append(("u",))
    out.append(("Us", 0))
    for t, items in ((0, ("kv", "ki", "q")), (1, ("kv",)), (0, ("kT", "qiT", "qT")), (1, ("ki",)),
                     (0, ("ix0", "ix1", "ix2", "ix3")), (1, ("q", "kT", "qiT", "ix0", "ix1", "ix2", "ix3"))):
        out.extend(project("dsa", t, *items))
    extra = {}
    for t in range(NT):
        if t + 2 < NT:
            at = {0: ("kv",), 1: ("ki",), 2: ("q",), 4: ("kT",), 5: ("qiT",),
                  7: ("qT", "ix0", "ix1", "ix2", "ix3")}
            if t + 2 == NT - 1:
                at[3] = ("cache",)
            merged(extra, {(t, s): project("dsa", t + 2, *i) for s, i in at.items()})
        if t > 0:
            merged(extra, {(t, 4): [("O", "dsa", t - 1)]})
    merged(extra, {(0, 0): project("dsa", 1, "qT"), (0, 1): [("Uv", 0), ("Us", 1)], (0, 3): [("Ub", 0)],
                   (0, 5): [("Uv", 1), ("Us", 2)], (0, 7): [("Ub", 1)], (1, 2): [("Uv", 2), ("Us", 3)],
                   (1, 4): [("Ub", 2)], (1, 6): [("Uv", 3)], (2, 0): [("Ub", 3)],
                   (3, 1): [("y", 0, 0, 0)], (3, 3): [("y", 0, 0, 1)],
                   (3, 5): [("y", 0, 1, 0), ("N", 1, 0)], (3, 6): [("y", 0, 1, 1), ("X", 1, 0)],
                   (3, 7): [("N", 1, 1), ("T", 1, 0)],
                   (4, 0): [("X", 1, 1)], (4, 1): [("y", 0, 2, 0), ("T", 1, 1)], (4, 3): [("y", 0, 2, 1)],
                   (4, 5): [("N", 1, 2), ("y", 0, 3, 0)], (4, 6): [("X", 1, 2)], (5, 0): [("T", 1, 2)]})
    stream("dsa", extra)
    out.extend(last_rows(0, "dsa"))
    out.extend([("lambda",)])
    items = {1: ("k",), 2: ("q",), 3: ("v",), 4: ("kT",), 5: ("qT",)}
    for t in range(NT + 1):
        if t < NT:
            out.extend([("C", 0, t), ("N", 2, t)])
        if t > 0:
            out.extend([("X", 2, t - 1), ("T", 2, t - 1), *project("sb", 0, *items[t])])
    extra = {}
    for t in range(NT):
        if t + 1 < NT:
            at = {0: ("k",), 1: ("v",), 3: ("q",), 4: ("kT",), 5: ("qT",)}
            if t + 1 == NT - 1:
                at[2] = ("cache",)
            merged(extra, {(t, s): project("sb", t + 1, *i) for s, i in at.items()})
        else:
            at = {0: ("k",), 2: ("q",), 3: ("kT",), 4: ("v",), 6: ("qT",)}
            merged(extra, {(t, s): project("diff", 0, *i) for s, i in at.items()})
        if t > 0:
            merged(extra, {(t, 6): [("O", "sb", t - 1)]})
    merged(extra, {(5, 0): project("diff", 1, "k"), (5, 1): project("diff", 1, "v"),
                   (5, 2): project("diff", 1, "q")})
    stream("sb", extra)
    out.append(("O", "sb", 4))
    out.extend(project("diff", 1, "kT", "qT"))
    extra = {}
    for t in range(NT):
        if t > 0:
            merged(extra, {(t + 1, 0) if t < 4 else (t, 3): [("O", "diff", t - 1)]})
        if t + 2 < NT:
            at = {0: ("k", "v"), 1: ("q",), 2: ("kT",), 3: ("qT",)}
            merged(extra, {(t, s): project("diff", t + 2, *i) for s, i in at.items()})
            if t + 2 == NT - 1:
                merged(extra, {(t, 1): project("diff", t + 2, "cache")})
    merged(extra, {(3, 0): [("y", 1, 0, 0)], (3, 1): [("y", 1, 0, 1), ("N", 3, 0)],
                   (3, 2): [("y", 1, 1, 0), ("X", 3, 0)], (3, 3): [("y", 1, 1, 1), ("N", 3, 1), ("T", 3, 0)],
                   (4, 0): [("X", 3, 1), ("y", 1, 2, 0)], (4, 1): [("y", 1, 2, 1), ("N", 3, 2), ("T", 3, 1)],
                   (4, 2): [("X", 3, 2)], (4, 3): [("T", 3, 2)], (5, 1): [("y", 1, 3, 0)]})
    stream("diff", extra)
    out.extend(last_rows(1, "diff"))
    for t in range(NT + 1):
        if t < NT:
            out.extend([("C", 1, t), ("N", 4, t)])
        if t > 0:
            out.extend([("X", 4, t - 1), ("Z", t - 1)])
    placed, due = [], []
    for step in out:
        while due and (step[0] == "router" or len(placed) >= due[0][0]):
            placed.append(due.pop(0)[1])
        placed.append(step)
        if step[0] == "T" and step[1] in (1, 3):
            due.append((len(placed) + 2, ("R", step[1] // 2, step[2])))
    return placed


def bank_plan(steps):
    plan = []
    for kind, *a in steps:
        if kind == "T":
            plan += [(("xT", *a, j), "dve") for j in range(2)]
        elif kind == "u":
            plan += [(("u", f), "act") for f in range(4)]
            plan += [((x,), "act") for x in ("us", "hist", "pool_p", "pool_s")]
        elif kind == "P":
            mech, t, item = a
            if item == "cache":
                plan += [((mech, "cache", b), "act") for b in range(2)]
            else:
                on_dve = item in ("kv", "ki", "q") or (mech == "diff" and item == "k")
                plan.append(((mech, item, t), "dve" if on_dve else "act"))
        elif kind == "A":
            mech, g = a
            if g < NT * HEADS[mech]:
                plan += [((mech, "s", *divmod(g, HEADS[mech]), c), "dve")
                         for c in range(2 if mech == "diff" else 1)]
            if 0 <= g - LAG[mech] < NT * HEADS[mech]:
                plan.append(((mech, "pT", *divmod(g - LAG[mech], HEADS[mech])), "act"))
        elif kind == "O":
            plan.append(((a[0], "oT", a[1]), "act"))
        elif kind == "Ub":
            plan += [(("dsa", x, a[0]), "act") for x in ("a", "as")]
        elif kind == "y":
            plan.append((("y", *a), "dve"))
        elif kind == "router":
            plan += [((x, a[0]), "dve") for x in ("rank", "list")]
        elif kind == "R":
            plan.append((("router", *a), "dve"))
    return plan


def stream_kernel(nc, x_prompt, x_sample, cache_pool, cache_dsa_k, cache_dsa_v, cache_idx_k, cache_sb_k,
                  cache_sb_v, cache_diff_k, cache_diff_v, norm_mix, norm_ffn, norm_final, w_in_even, w_pool,
                  pool_scale, w_out_even, w_in_odd, diff_lambda, diff_subln, w_out_odd, moe_w_group,
                  moe_b_group, moe_w_expert, moe_b_expert, moe_w1, moe_w3, moe_w2, constants,
                  y_prompt, y_sample, pool_p, dsak_p, dsav_p, idxk_p, sbk_p, sbv_p, dfk_p, dfv_p,
                  pool_s, dsak_s, dsav_s, idxk_s, sbk_s, sbv_s, dfk_s, dfv_s):
    steps = schedule()
    plan = bank_plan(steps)
    NB = 6
    number = {key: i for i, (key, _) in enumerate(plan)}
    reader = dict(plan)
    rank, last_rank = {}, {"act": 0, "dve": 0}
    for key, who in plan:
        last_rank[who] += 1
        rank[key] = last_rank[who]

    ctx = ExitStack()
    with ctx:
        def sb(name, shape, dt=F32):
            return ctx.enter_context(nc.sbuf_tensor(name, shape, dt))

        def sem(name):
            return ctx.enter_context(nc.semaphore(name))

        h = sb("h", [P, NT, DM])
        normed = sb("normed", [P, NT * DM])
        xT = sb("xT", [P, KC, NTOK])
        slot = sb("slot", [P, 6, 4096])
        const = sb("const", [P, C_N])
        params = sb("params", [P, 664])
        stats = sb("stats", [P, 640])
        arena = sb("arena", [P, 11040])

        mixT = normed[:, 0:8 * NTOK].rearrange("p (f n) -> p f n", f=8)
        spare = normed[:, 8 * NTOK:NT * DM]
        cos = const[:, C_COS:C_COS + 160].rearrange("p (t e) -> p t e", t=NT)
        sin = const[:, C_SIN:C_SIN + 160].rearrange("p (t e) -> p t e", t=NT)
        ident = const[:, C_ID:C_ID + P]

        g_norm = params[:, 0:32].rearrange("p (n k) -> p n k", n=4)
        w_router = params[:, 32:352].rearrange("p (l k n) -> p l k n", l=2, k=KC)
        b_router = params[:, 352:392].rearrange("p (l n) -> p l n", l=2)
        scale_pool = params[:, 392:396]
        gain_diff = params[:, 396:397]
        gain_out = params[:, 397:398]
        lam_in = params[:, 400:656]
        lam_dot = params[:, 656:658]
        lam_exp = params[:, 658:660]
        lam = params[:, 660:661]

        ssq = stats[:, 0:25].rearrange("p (n t) -> p n t", n=5)
        root = stats[:, 25:50].rearrange("p (n t) -> p n t", n=5)
        logm = stats[:, 50:75].rearrange("p (n t) -> p n t", n=5)
        rstd = stats[:, 75:100].rearrange("p (n t) -> p n t", n=5)
        least = stats[:, 100:116]
        rowsum = stats[:, 116:132]
        rinv = stats[:, 132:148]
        newton = stats[:, 360:361]
        newton_m = stats[:, 361:362]
        top8 = stats[:, 148:156]
        w_idx = stats[:, 156:164].rearrange("p (r c) -> p r c", r=2)
        rlam = stats[:, 148:149]
        osq = stats[:, 164:168]
        oms = stats[:, 168:172]
        oln = stats[:, 172:176]
        ors = stats[:, 176:180]
        logits = stats[:, 180:280].rearrange("p (t n) -> p t n", t=NT)
        gate = stats[:, 280:360].rearrange("p (t n) -> p t n", t=NT)
        route = stats[:, 364:640]

        r_exp = route[:, 0:25]
        r_arg = route[:, 25:50]

        at = 0

        def area(n):
            nonlocal at
            at += n
            return arena[:, at - n:at]

        kT = area(4 * NKEY).rearrange("p (f n) -> p f n", f=4)
        values = area(7 * 512)
        qT = area(1024).rearrange("p (r f n) -> p r f n", r=2, f=4)
        rows = area(1152)
        ropeA = area(512)
        ropeB = area(512)
        lo, hi = slot[:, 3, :], slot[:, 5, :]
        crow = lo[:, 0:1024].rearrange("p (b n) -> p b n", b=2)
        score = lo[:, 1024:2048].rearrange("p (r n) -> p r n", r=2)
        prob = lo[:, 2048:3072].rearrange("p (r n) -> p r n", r=2)
        probT = lo[:, 3072:4096].rearrange("p (r b n) -> p r b n", r=2, b=4)
        orow = hi[:, 0:1024].rearrange("p (r n) -> p r n", r=2)
        idxrel = hi[:, 1024:1536]
        idxacc = hi[:, 1536:2048]
        pooled = hi[:, 2048:2560]
        pooled_s = spare[:, UEXT:UEXT + DEC]
        selected = hi[:, 2560:3584].rearrange("p (r n) -> p r n", r=2)
        wpool = hi[:, 3584:4096].rearrange("p (g n) -> p g n", g=4)
        kiw = area(KC * KIW).rearrange("p (k n) -> p k n", k=KC)
        qiT = area(512).rearrange("p (r f n) -> p r f n", r=2, f=2)
        uT = values[:, 896:896 + 4 * UEXT].rearrange("p (g n) -> p g n", g=4)
        sumA = spare[:, 0:UEXT]
        sumB = kT[:, 3, 0:UEXT]
        logp = hi[:, 1024:2048].rearrange("p (r n) -> p r n", r=2)
        tail = hi[:, 2048:3072].rearrange("p (r n) -> p r n", r=2)
        expo = hi[:, 1024:3072].rearrange("p (r n) -> p r n", r=4)
        odd_junk = hi[:, 3072:3584]
        vdsa = values[:, 0:896].rearrange("p (b n) -> p b n", b=7)
        vodd = values.rearrange("p (b n) -> p b n", b=7)
        hid = arena[:, 0:4 * NTOK].rearrange("p (m n) -> p m n", m=4)
        silu = arena[:, 4 * NTOK:6 * NTOK].rearrange("p (r s n) -> p r s n", r=2, s=2)
        xg = arena[:, 0:3072].rearrange("p (r d) -> p r d", r=3)
        xgT = arena[:, 3072:4608].rearrange("p (r k n) -> p r k n", r=2, k=KC)
        gsilu = arena[:, 4608:4992]
        ghid = arena[:, 5120:5888].rearrange("p (r m n) -> p r m n", r=2, m=4)
        yrow = arena[:, 5888:7936].rearrange("p (r d) -> p r d", r=2)
        first_y = normed[:, :].rearrange("p (t d) -> p t d", t=NT)
        second_y = arena[:, 0:5120].rearrange("p (t d) -> p t d", t=NT)
        upto = arena[:, 8000:8128]
        ones = arena[:, 8128:8256]
        chosen = arena[:, 8256:8416].rearrange("p (c n) -> p c n", c=2)
        mask = arena[:, 8416:8496]
        place = arena[:, 8496:8576]
        spot = arena[:, 8576:8656]
        picked = arena[:, 8656:8816].rearrange("p (c n) -> p c n", c=2)
        at_place = arena[:, 8816:9776].rearrange("p (c n) -> p c n", c=2 * NT)
        token_at = arena[:, 9776:9936].rearrange("p (c n) -> p c n", c=2 * NT)
        place_c = arena[:, 9936:9946]
        spot_c = arena[:, 9946:9956]
        most = arena[:, 9956:9957]
        tokens_of = arena[:, 9960:9976].bitcast(U32)
        y_rows = arena[:, 9976:9986].bitcast(U32)
        most_int = arena[:, 9988:9989].bitcast(I32)
        xn_of = [(slot[:, 1, 0:3 * DM] if n in (1, 3) else lo[:, 1024:4096]).rearrange("p (r d) -> p r d", r=3)
                 for n in range(5)]
        junk_of = [slot[:, 1, 3 * DM:4 * DM] if n in (1, 3) else hi[:, 0:DM] for n in range(5)]
        fin = normed[:, :].rearrange("p (t d) -> p t d", t=NT)
        gfin = slot[:, 0, 0:DM]
        lam_tmp = crow[:, 1, 0:HD]
        histrow = ropeA
        poolout = ropeB

        bank = ctx.enter_context(nc.psum_tensor("bank", [P, 8, 512], F32))

        x_dram = [nc.dram_tensor(f"normed_rows{l}", [NTOK, DM], F32, kind="Internal").ap() for l in range(2)]
        y_dram = [nc.dram_tensor(f"expert_rows{l}", [NE * CAP, DM], F32, kind="Internal").ap()
                  for l in range(2)]

        x_in = [sem(f"x_in{t}") for t in range(NT)]
        const_in = sem("const_in")
        gain_in = sem("gain_in")
        small_in = sem("small_in")
        slot_in = [sem(f"slot{s}_in") for s in range(6)]
        kiw_in = sem("kiw_in")
        wpool_in = sem("wpool_in")
        hist_in = sem("hist_in")
        krow_in = sem("krow_in")
        vrow_in = sem("vrow_in")
        w13_in = [[sem(f"{q}_w13_in{l}") for q in ("even", "odd")] for l in range(2)]
        w2_in = [[sem(f"{q}_w2_in{l}") for q in ("even", "odd")] for l in range(2)]
        gfin_in = sem("gfin_in")
        bank_filled = sem("bank_filled")
        bank_read = {"act": sem("bank_read_act"), "dve": sem("bank_read_dve")}
        out_filled = sem("out_filled")
        out_read = sem("out_read")
        squared = sem("squared")
        root_ready = sem("root_ready")
        xn_ready = sem("xn_ready")
        zeros_set = sem("zeros_set")
        rope_out = sem("rope_out")
        index_ready = sem("index_ready")
        abs_ready = sem("abs_ready")
        soft_ready = sem("soft_ready")
        tail_ready = sem("tail_ready")
        expo_in = sem("expo_in")
        exp_done = sem("exp_done")
        prob_ready = sem("prob_ready")
        osq_ready = sem("osq_ready")
        ors_ready = sem("ors_ready")
        sums_ready = sem("sums_ready")
        pooled_ready = sem("pooled_ready")
        lam_dots = sem("lam_dots")
        lam_exps = sem("lam_exps")
        out_rows = sem("out_rows")
        out_vals = sem("out_vals")
        out_pool = sem("out_pool")
        out_y = sem("out_y")
        route_in = sem("route_in")
        route_exp = sem("route_exp")
        moe_g = [sem(f"moe_g{l}") for l in range(2)]
        moe_u = [sem(f"moe_u{l}") for l in range(2)]
        moe_y = [sem(f"moe_y{l}") for l in range(2)]
        silu_done = [sem(f"silu_done{l}") for l in range(2)]
        hid_done = [sem(f"hid_done{l}") for l in range(2)]
        y_added = [sem(f"y_added{l}") for l in range(2)]
        x_stored = [[sem(f"x_stored{l}{r}") for r in range(3)] for l in range(2)]
        xg_in = [[sem(f"xg_in{l}{r}") for r in range(3)] for l in range(2)]
        xg_turned = [sem(f"xg_turned{l}") for l in range(2)]
        xgT_ready = [sem(f"xgT_ready{l}") for l in range(2)]
        up_done = [sem(f"up_done{l}") for l in range(2)]
        gsilu_done = [sem(f"gsilu_done{l}") for l in range(2)]
        ghid_done = [sem(f"ghid_done{l}") for l in range(2)]
        down_done = [sem(f"down_done{l}") for l in range(2)]
        yrow_ready = [sem(f"yrow_ready{l}") for l in range(2)]
        y_stored = [[sem(f"y_stored{l}{r}") for r in range(2)] for l in range(2)]
        picked_in = [[sem(f"picked_in{l}{t}") for t in range(NT)] for l in range(2)]
        h_added = sem("h_added")
        lists_in = sem("lists_in")
        mask_ready = sem("mask_ready")
        gained = sem("gained")
        scale_ready = sem("scale_ready")
        fin_ready = sem("fin_ready")
        act_step = sem("act_step")
        dve_step = sem("dve_step")
        pool_step = sem("pool_step")

        block = ctx.enter_context(nc.Block())

        def crowded(eng, l):
            taken(eng, ("list", l))
            return eng.value_load(most_int[0:1, 0:1], min_val=0, max_val=NTOK) > CAP

        def filled(eng, key):
            eng.wait_ge(bank_filled, number[key] + 1)
            return bank[:, number[key] % NB, :]

        def taken(eng, key):
            eng.wait_ge(bank_read[reader[key]], rank[key])

        def all_x_stored(eng, l):
            for r in range(3):
                eng.wait_ge(x_stored[l][r], 16 * len(range(r, NT, 3)))

        MECHS = ("dsa", "sb", "diff")
        tiles_before = {m: NT * i for i, m in enumerate(MECHS)}
        heads_before = {"dsa": 0, "sb": 8 * NT, "diff": 16 * NT}
        maps_before = heads_before

        def head_no(mech, t, hd):
            return heads_before[mech] + t * HEADS[mech] + hd

        def map_no(mech, t, hd, c):
            n = 2 if mech == "diff" else 1
            return maps_before[mech] + (t * HEADS[mech] + hd) * n + c

        heads = [(m, "pT", t, hd) for m in MECHS for t in range(NT) for hd in range(HEADS[m])]

        def prob_of(mech, n):
            m = n - heads_before[mech]
            return odd_junk if mech == "sb" and m % 3 == 2 else prob[:, m % 3 if mech == "sb" else m % 2, :]

        def prob_turned(eng, mech, n):
            first, ring = heads_before[mech], 3 if mech == "sb" else 2
            last = n - ring if n - ring >= first else first - 1
            eng.wait_ge(bank_filled, number[heads[last]] + 1)

        def xn(n, t):
            return xn_of[n][:, t % 3, :]

        def rope_no(mech, t, part):
            return (0 if mech == "dsa" else 2 * NT) + 2 * t + part

        def rows2d(ap):
            return ap.rearrange("a b s g d -> (a b s) (g d)")

        @block.sync
        def _(sp):
            sp.dma_start(h[:, 0, :], x_prompt[0, 0:P]).then_inc(x_in[0], 16)
            sp.dma_start(const[:, :], constants).then_inc(const_in, 16)
            for t in range(1, 4):
                sp.dma_start(h[:, t, :], x_prompt[0, P * t:P * t + P]).then_inc(x_in[t], 16)
            sp.dma_start(h[0:DEC, 4, :], x_sample[0]).then_inc(x_in[4], 16)
            w_even = w_in_even[0].rearrange("(p k) n -> p k n", k=KC)
            for s, c in ((S_U, 0), (S_KV, 1024), (S_Q, 512)):
                sp.dma_start(slot[:, s, :].rearrange("p (k n) -> p k n", k=KC), w_even[:, :, c:c + 512])\
                  .then_inc(slot_in[s], 16)
                if s == S_U:
                    sp.dma_start(histrow[0:HIST, :], cache_pool[0, 0]).then_inc(hist_in, 16)
                    sp.dma_start(kiw, w_even[:, :, 1536:1536 + KIW]).then_inc(kiw_in, 16)
            sp.dma_start(wpool, w_pool[0].rearrange("g c n -> c g n")).then_inc(wpool_in, 16)
            ck = crow[:, :, 0:256].rearrange("p b (g u d) -> p b g u d", g=2, u=2)
            for b in range(2):
                for u in range(2):
                    sp.dma_start(ck[:, b, :, u, :], cache_dsa_k[0, 0, P * b:P * b + P]).then_inc(krow_in, 16)
                    sp.dma_start(crow[:, b, 256 + HD * u:256 + HD * u + HD],
                                 cache_idx_k[0, 0, P * b:P * b + P]).then_inc(krow_in, 16)
                sp.dma_start(vdsa[:, 4 + b, :], cache_dsa_v[0, 0, P * b:P * b + P]
                             .rearrange("p g d -> p (g d)")).then_inc(vrow_in, 16)

            for n, g in ((1, norm_ffn[0]), (2, norm_mix[1]), (3, norm_ffn[1])):
                sp.dma_start(g_norm[:, n, :], g.rearrange("(p k) -> p k", k=KC)).then_inc(small_in, 16)
            with nc.allow_non_contiguous_dma(reason="a few columns of parameters"):
                sp.dma_start(scale_pool, pool_scale[0].rearrange("(g p) -> p g", p=P)).then_inc(small_in, 16)
                sp.dma_start(gain_diff, diff_subln[0].rearrange("(p a) -> p a", a=1)).then_inc(small_in, 16)
                for l in range(2):
                    sp.dma_start(w_router[:, l, :, 0:4], moe_w_group[l].rearrange("(p k) n -> p k n", k=KC))\
                      .then_inc(small_in, 16)
                    for g in range(4):
                        sp.dma_start(w_router[:, l, :, 4 + 4 * g:8 + 4 * g],
                                      moe_w_expert[l, g].rearrange("(p k) n -> p k n", k=KC))\
                          .then_inc(small_in, 16)
            for l in range(2):
                sp.dma_start(b_router[:, l, 0:4], moe_b_group[l].partition_broadcast(P)).then_inc(small_in, 16)
                sp.dma_start(b_router[:, l, 4:20], moe_b_expert[l].rearrange("g n -> (g n)")
                              .partition_broadcast(P)).then_inc(small_in, 16)
            sp.dma_start(lam_in, diff_lambda[0].rearrange("a n -> (a n)").partition_broadcast(P))\
               .then_inc(small_in, 16)

            def w_out_load(w, slots, waits):
                for j in range(2):
                    waits[j]()
                    sp.dma_start(slot[:, slots[j], :].rearrange("p (k n) -> p k n", k=4),
                                 w[0].rearrange("(k p) n -> p k n", p=P)[:, 4 * j:4 * j + 4, :])\
                      .then_inc(slot_in[slots[j]], 16)

            w_out_load(w_out_even, OUT_EVEN, (lambda: sp.wait_ge(bank_filled, number[("us",)] + 1),
                                              lambda: None))

            def w_load(w, s, l, e, par):
                sp.dma_start(slot[:, s, :].rearrange("p (k n) -> p k n", k=KC),
                             w[l, e].rearrange("(p k) n -> p k n", k=KC)).then_inc(w13_in[l][par], 16)

            def w13_load(l, e, par, first=None):
                for w, s in ((moe_w3, W3), (moe_w1, W1)):
                    if first:
                        first(s[par])
                    w_load(w, s[par], l, e, par)

            def w2_load(l, e, par, first=None):
                if first:
                    first(W2[par])
                sp.dma_start(slot[:, W2[par], :].rearrange("p (k n) -> p k n", k=4),
                             moe_w2[l, e].rearrange("(k p) n -> p k n", p=P)).then_inc(w2_in[l][par], 16)

            def experts(l, first, then=()):
                w13_load(l, 0, 0, first)
                w2_load(l, 0, 0, first)
                first(W3[1])
                w_load(moe_w3, W3[1], l, 1, 1)
                full = crowded(sp, l)
                with sp.If(full):
                    first(W1[1])
                    w_load(moe_w1, W1[1], l, 1, 1)
                    w2_load(l, 1, 1, first)
                    with sp.Fori(0, NE // 2 - 1) as i:
                        for par in range(2):
                            sp.wait_ge(moe_y[l], (2 * i + par + 1) * NT)
                            w13_load(l, 2 * i + 2 + par, par)
                            w2_load(l, 2 * i + 2 + par, par)
                    sp.wait_ge(moe_y[l], NE * NT)
                    for load in then:
                        load()
                with sp.Else():
                    first(W1[1])
                    sp.wait_ge(xg_turned[l], 1)
                    w_load(moe_w1, W1[1], l, 1, 1)
                    w2_load(l, 1, 1, first)
                    def up_weights(e, par):
                        sp.wait_ge(up_done[l], e - 1)
                        w13_load(l, e, par)

                    def down_weights(e, par):
                        sp.wait_ge(down_done[l], e - 1)
                        w2_load(l, e, par)

                    up_weights(2, 0)
                    with sp.Fori(0, NE // 2 - 2) as i:
                        for par in range(2):
                            up_weights(2 * i + par + 3, 1 - par)
                            down_weights(2 * i + par + 2, par)
                    up_weights(NE - 1, 1)
                    down_weights(NE - 2, 0)
                    down_weights(NE - 1, 1)
                    sp.wait_ge(up_done[l], NE - 1)
                    for load in then[0:2]:
                        load()
                    sp.wait_ge(down_done[l], NE - 1)
                    for load in then[2:]:
                        load()
                    sp.wait_ge(down_done[l], NE)

            def mixer_left(layer, mech, freed):
                def wait(s):
                    key = freed.get(s)
                    sp.wait_ge(bank_filled, number[key] + 1)
                    if s == 1:
                        n = 2 * layer + 1
                        sp.wait_ge(bank_filled, number[("xT", n, NT - 1, 1)] + 1)
                        all_x_stored(sp, layer)
                    if s in (3, 5):
                        sp.wait_ge(out_read, tiles_before[mech] + NT)
                        taken(sp, (mech, "oT", NT - 1))
                return wait

            def odd_load(s, c, then):
                if then:
                    sp.wait_ge(bank_filled, number[then] + 1)
                sp.dma_start(slot[:, s, :].rearrange("p (k n) -> p k n", k=KC),
                             w_in_odd[0].rearrange("(p k) n -> p k n", k=KC)[:, :, 512 * c:512 * c + 512])\
                  .then_inc(slot_in[s], 16)

            left = ("y", 0, NT - 1, 1)
            experts(0, mixer_left(0, "dsa", {1: ("dsa", "q", 4), 2: ("dsa", "kv", 4), 0: left, 4: left,
                                             3: left, 5: left}),
                    (lambda: odd_load(SB_K, 1, None), lambda: odd_load(SB_V, 2, None),
                     lambda: odd_load(SB_Q, 0, None)))

            def cache_load(k, v, mech):
                for b in range(2):
                    src_k, src_v = k[0, 0, P * b:P * b + P], v[0, 0, P * b:P * b + P]
                    src_k = src_k.rearrange("p g d -> p (g d)") if mech == "sb" else \
                        src_k.rearrange("p g c d -> p (g c d)")
                    sp.dma_start(crow[:, b, :], src_k).then_inc(krow_in, 16)
                    sp.dma_start(vodd[:, 4 + b, :], src_v.rearrange("p g d -> p (g d)")).then_inc(vrow_in, 16)

            sp.wait_ge(h_added, 2 * NT)
            cache_load(cache_sb_k, cache_sb_v, "sb")
            odd_load(DF_K, 4, None)
            odd_load(DF_V, 5, ("sb", "k", 4))
            odd_load(DF_Q, 3, ("sb", "v", 4))
            def after_sb():
                sp.wait_ge(bank_filled, number[("sb", "q", 4)] + 1)

            def after_diff_k():
                sp.wait_ge(out_filled, head_no("sb", 4, 7) + 1)
                cache_load(cache_diff_k, cache_diff_v, "diff")
                sp.wait_ge(bank_filled, number[("diff", "k", 4)] + 1)

            w_out_load(w_out_odd, OUT_ODD, (after_sb, after_diff_k))
            left = ("y", 1, NT - 1, 1)
            experts(1, mixer_left(1, "diff", {1: ("diff", "v", 4), 2: ("diff", "q", 4), 0: left, 4: left,
                                              3: left, 5: left}))
            sp.dma_start(gfin, norm_final.partition_broadcast(P)).then_inc(gfin_in, 16)
            for t in range(NT):
                sp.wait_ge(fin_ready, t + 1)
                dst = y_prompt[0, P * t:P * t + P, :] if t < 4 else y_sample[0]
                sp.dma_start(dst, fin[0:ROWS[t], t, :]).then_inc(out_y, 16)
            sp.wait_ge(out_y, 16 * NT)
            sp.wait_ge(out_rows, 16 * (2 + 1 + 1) * NT)
            sp.wait_ge(out_vals, 16 * 3 * NT)
            sp.wait_ge(out_pool, 32)

        @block.tensor
        def _(pe):
            turn = [0]

            def fill(key):
                i = number[key]
                assert turn[0] == i, (key, plan[turn[0]])
                turn[0] += 1
                if i >= NB:
                    taken(pe, plan[i - NB][0])
                return bank[:, i % NB, :]

            def weights(s, n=KC):
                return slot[:, s, :].rearrange("p (k n) -> p k n", k=n)

            def step_T(n, t):
                pe.wait_ge(xn_ready, NT * n + t + 1)
                r = ROWS[t]
                src = xn(n, t)[0:r, :].rearrange("r (p k) -> r k p", k=KC)
                for j in range(2):
                    b = fill(("xT", n, t, j))
                    for k in range(4):
                        last = nc.tensor.transpose(b[:, P * k:P * k + r], src[:, 4 * j + k, :],
                                                   ident[0:r, 0:r])
                    last.then_inc(bank_filled, 1)

            def xT_ready(n, t):
                taken(pe, ("xT", n, t, 1))

            def project(key, t, w, n):
                b = fill(key)
                for k in range(KC):
                    last = nc.tensor.matmul(b[0:ROWS[t], 0:n], xT[:, k, tok(t)], w[:, k, 0:n],
                                            start=(k == 0), stop=(k == KC - 1))
                last.then_inc(bank_filled, 1)

            def transposes(key, srcs, r):
                b = fill(key)
                for i, s in enumerate(srcs):
                    last = nc.tensor.transpose(b[0:s.shape[1], P * i:P * i + r], s, ident[0:r, 0:r])
                last.then_inc(bank_filled, 1)

            def step_u():
                pe.wait_ge(slot_in[S_U], 16)
                for f in range(4):
                    b = fill(("u", f))
                    if f == 0:
                        xT_ready(0, NT - 1)
                    for k in range(KC):
                        last = nc.tensor.matmul(b[:, :], weights(S_U)[:, k, P * f:P * f + P], xT[:, k, 0:SEQ],
                                                start=(k == 0), stop=(k == KC - 1))
                    last.then_inc(bank_filled, 1)
                b = fill(("us",))
                for f in range(4):
                    for k in range(KC):
                        last = nc.tensor.matmul(b[:, DEC * f:DEC * f + DEC],
                                                weights(S_U)[:, k, P * f:P * f + P], xT[:, k, SEQ:NTOK],
                                                start=(k == 0), stop=(k == KC - 1))
                last.then_inc(bank_filled, 1)
                b = fill(("hist",))
                pe.wait_ge(hist_in, 16)
                for f in range(4):
                    last = nc.tensor.transpose(b[:, 16 * f:16 * f + HIST], histrow[0:HIST, P * f:P * f + P],
                                               ident[0:HIST, 0:HIST])
                last.then_inc(bank_filled, 1)
                for key, c in ((("pool_p",), SEQ), (("pool_s",), UEXT - HIST)):
                    b = fill(key)
                    taken(pe, ("us",))
                    for f in range(4):
                        last = nc.tensor.transpose(b[0:HIST, P * f:P * f + P], uT[:, f, c:c + HIST], ident)
                    last.then_inc(bank_filled, 1)

            def step_P(mech, t, item):
                r = ROWS[t]
                if item == "cache":
                    for b in range(2):
                        pe.wait_ge(krow_in, {"dsa": 128, "sb": 160, "diff": 192}[mech])
                        n = 3 if mech == "dsa" else 4
                        transposes((mech, "cache", b), [crow[:, b, P * i:P * i + P] for i in range(n)], P)
                elif item in ("kv", "k", "v", "q"):
                    s = {"dsa": {"kv": S_KV, "q": S_Q}, "sb": {"k": SB_K, "v": SB_V, "q": SB_Q},
                         "diff": {"k": DF_K, "v": DF_V, "q": DF_Q}}[mech][item]
                    if t == 0:
                        pe.wait_ge(slot_in[s], slot_count(s, mech))
                    xT_ready(0 if mech == "dsa" else 2, t)
                    project((mech, item, t), t, weights(s), 512)
                elif item == "ki":
                    if t == 0:
                        pe.wait_ge(kiw_in, 16)
                    project((mech, item, t), t, kiw, KIW)
                elif item in ("kT", "qiT", "qT"):
                    if mech == "sb":
                        taken(pe, (mech, item[0], t))
                    else:
                        pe.wait_ge(rope_out, rope_no(mech, t, 1 if item == "qT" else 0) + 1)
                    cols = {"dsa": {"kT": (0, 1, 4), "qiT": (2, 3), "qT": (5, 6, 7, 8)}}.get(
                        mech, {"kT": (0, 1, 2, 3), "qT": (4, 5, 6, 7)})[item]
                    transposes((mech, item, t), [rows[0:r, P * i:P * i + P] for i in cols], r)
                else:
                    hd = int(item[2])
                    k0, nk, _ = keys_at(t)
                    b = fill((mech, item, t))
                    if hd == 0:
                        taken(pe, (mech, "qiT", t))
                    o = HD * (hd % 2)
                    nc.tensor.matmul(b[0:r, 0:nk], qiT[o:o + HD, t % 2, hd // 2, 0:r],
                                     kT[o:o + HD, 2, k0:k0 + nk], start=True, stop=True)\
                      .then_inc(bank_filled, 1)

            def step_A(mech, g):
                count = HEADS[mech]
                if g < NT * count:
                    t, hd = divmod(g, count)
                    r = ROWS[t]
                    k0, nk, _ = keys_at(t)
                    tile = tiles_before[mech] + t
                    if hd == 0:
                        taken(pe, (mech, "qT", t))
                        taken(pe, (mech, "kT", t))
                        if t == NT - 1:
                            taken(pe, (mech, "cache", 1))
                    for c in range(2 if mech == "diff" else 1):
                        b = fill((mech, "s", t, hd, c))
                        if mech == "diff":
                            o, f, kf = HD * c, hd, hd
                        else:
                            o, f = HD * (hd % 2), hd // 2
                            kf = hd // 4 if mech == "dsa" else f
                        nc.tensor.matmul(b[0:r, 0:nk], qT[o:o + HD, tile % 2, f, 0:r],
                                         kT[o:o + HD, kf, k0:k0 + nk], start=True, stop=True)\
                          .then_inc(bank_filled, 1)
                if 0 <= g - LAG[mech] < NT * count:
                    t, hd = divmod(g - LAG[mech], count)
                    r, n = ROWS[t], head_no(mech, t, hd)
                    b = fill((mech, "pT", t, hd))
                    pe.wait_ge(prob_ready, n + 1)
                    for i, (_, kr) in enumerate(key_blocks(t)):
                        last = nc.tensor.transpose(b[0:kr, P * i:P * i + r],
                                                   prob_of(mech, n)[0:r, P * i:P * i + kr], ident[0:r, 0:r])
                    last.then_inc(bank_filled, 1)
                if 0 <= g - LAG[mech] - 1 < NT * count:
                    t, hd = divmod(g - LAG[mech] - 1, count)
                    r, n = ROWS[t], head_no(mech, t, hd)
                    tile = tiles_before[mech] + t
                    blocks = key_blocks(t)
                    if hd == 0:
                        if tile >= 2:
                            pe.wait_ge(out_read, tile - 1)
                        if mech == "dsa":
                            taken(pe, (mech, "kv", t))
                        else:
                            taken(pe, (mech, "v", t))
                        if t == NT - 1:
                            pe.wait_ge(vrow_in, {"dsa": 32, "sb": 64, "diff": 96}[mech])
                    taken(pe, (mech, "pT", t, hd))
                    vals, w, c = {"dsa": (vdsa, HD, HD * (hd // 4)), "sb": (vodd, HD, HD * hd),
                                  "diff": (vodd, P, P * hd)}[mech]
                    out = bank[:, NB + tile % 2, :]
                    for i, (vb, kr) in enumerate(blocks):
                        last = nc.tensor.matmul(out[0:r, w * hd:w * hd + w], probT[0:kr, n % 2, i, 0:r],
                                                vals[0:kr, vb, c:c + w], start=(i == 0),
                                                stop=(i == len(blocks) - 1))
                    last.then_inc(out_filled, 1)

            def step_O(mech, t):
                tile = tiles_before[mech] + t
                pe.wait_ge(out_read, tile + 1)
                r = ROWS[t]
                transposes((mech, "oT", t), [orow[0:r, tile % 2, P * i:P * i + P] for i in range(4)], r)

            def step_U(g):
                if g == 0:
                    pe.wait_ge(wpool_in, 16)
                pe.wait_ge(pooled_ready, g + 1)
                for key, rhs, n in ((("dsa", "a", g), pooled, SEQ), (("dsa", "as", g), pooled_s, DEC)):
                    b = fill(key)
                    nc.tensor.matmul(b[:, 0:n], wpool[:, g, :], rhs,
                                     start=True, stop=True).then_inc(bank_filled, 1)

            def slot_count(s, mech):
                loads = {"dsa": (S_U, S_Q, S_KV), "out0": OUT_EVEN, "sb": (SB_K, SB_V, SB_Q),
                         "diff": (DF_K, DF_V, DF_Q), "out1": OUT_ODD}
                n = 0
                for name, slots in loads.items():
                    n += slots.count(s)
                    if name == mech:
                        return 16 * n

            def step_y(layer, t, j):
                slots = (OUT_EVEN, OUT_ODD)[layer]
                if t == 0 and j == 0:
                    for s in slots:
                        pe.wait_ge(slot_in[s], slot_count(s, f"out{layer}"))
                if layer == 1:
                    taken(pe, ("sb", "oT", t))
                    taken(pe, ("diff", "oT", t))
                else:
                    taken(pe, ("dsa", "as", 3))
                    taken(pe, ("dsa", "oT", t))
                b = fill(("y", layer, t, j))
                for k in range(KC):
                    w = weights(slots[k // 4], 4)
                    last = nc.tensor.matmul(b[0:ROWS[t], :], mixT[:, k, tok(t)],
                                            w[:, k % 4, 512 * j:512 * j + 512],
                                            start=(k == 0), stop=(k == KC - 1))
                last.then_inc(bank_filled, 1)

            def step_R(l, t):
                b = fill(("router", l, t))
                xT_ready(2 * l + 1, t)
                for k in range(KC):
                    last = nc.tensor.matmul(b[0:ROWS[t], 0:20], xT[:, k, tok(t)], w_router[:, l, k, :],
                                            start=(k == 0), stop=(k == KC - 1))
                last.then_inc(bank_filled, 1)

            def lists(l):
                b = fill(("rank", l))
                pe.wait_ge(mask_ready, l + 1)
                nc.tensor.matmul(b[:, 0:NE * NT], upto, mask, start=True, stop=False)
                for d in range(1, NT):
                    nc.tensor.matmul(b[:, NE * d:NE * NT], ones, mask[:, 0:NE * (NT - d)], start=False,
                                     stop=(d == NT - 1))
                for t in range(NT):
                    r = ROWS[t]
                    last = nc.tensor.matmul(b[:, NE * NT:NE * NT + NE], ones[0:r, :],
                                            mask[0:r, NE * t:NE * t + NE], start=(t == 0), stop=(t == NT - 1))
                last.then_inc(bank_filled, 1)
                b = fill(("list", l))
                pe.wait_ge(lists_in, l + 1)
                for t in range(NT):
                    r = ROWS[t]
                    for c in range(2):
                        last = nc.tensor.matmul(b[0:CAP, 0:NE], at_place[0:r, NT * c + t, :],
                                                token_at[0:r, NT * c + t, :],
                                                start=(t == 0 and c == 0), stop=(t == NT - 1 and c == 1))
                last.then_inc(bank_filled, 1)

            def experts(l):
                for who in ("act", "dve"):
                    pe.wait_ge(bank_read[who], max(rank[k] for k, v in plan[0:number[("list", l)] + 1]
                                                   if v == who))
                pe.wait_ge(out_read, NT if l == 0 else 3 * NT)
                full = crowded(pe, l)
                with pe.If(full):
                    all_tokens(l)
                with pe.Else():
                    own_tokens(l)

            def turn_rows(l, e, r3, par):
                pe.wait_ge(xg_in[l][r3], 16 * (e // 3) + 16)
                if e > 0:
                    pe.wait_ge(xgT_ready[l], e)
                for k in range(KC):
                    last = nc.tensor.transpose(bank[:, k // 4, CAP * (k % 4):CAP * (k % 4) + CAP],
                                               xg[0:CAP, r3, :].rearrange("r (p k) -> r k p", k=KC)[:, k, :],
                                               ident[0:CAP, 0:CAP])
                last.then_inc(xg_turned[l], 1)

            def up(l, e, par):
                pe.wait_ge(w13_in[l][par], 32 * (e // 2) + 32)
                pe.wait_ge(xgT_ready[l], e + 1)
                if e >= 2:
                    pe.wait_ge(ghid_done[l], e - 1)
                for w, b in ((W1, 2 + 2 * par), (W3, 3 + 2 * par)):
                    for m in range(4):
                        for k in range(KC):
                            last = nc.tensor.matmul(bank[:, b, CAP * m:CAP * m + CAP],
                                                    weights(w[par])[:, k, P * m:P * m + P],
                                                    xgT[:, par, k, :], start=(k == 0), stop=(k == KC - 1))
                last.then_inc(up_done[l], 1)

            def down(l, e, par):
                pe.wait_ge(w2_in[l][par], 16 * (e // 2) + 16)
                pe.wait_ge(ghid_done[l], e + 1)
                if e >= 1:
                    pe.wait_ge(yrow_ready[l], e)
                for j in range(2):
                    for m in range(4):
                        last = nc.tensor.matmul(bank[0:CAP, 6 + j, :], ghid[:, par, m, :],
                                                weights(W2[par], 4)[:, m, 512 * j:512 * j + 512],
                                                start=(m == 0), stop=(m == 3))
                last.then_inc(down_done[l], 1)

            def own_tokens(l):
                turn_rows(l, 0, 0, 0)
                for e in range(NE):
                    if e + 1 < NE:
                        turn_rows(l, e + 1, (e + 1) % 3, (e + 1) % 2)
                    up(l, e, e % 2)
                    if e > 0:
                        down(l, e - 1, (e - 1) % 2)
                down(l, NE - 1, (NE - 1) % 2)

            def all_tokens(l):
                with pe.Fori(0, NE // 2) as i:
                    for par in range(2):
                        expert_body(l, 2 * i + par, i, par)

            def expert_body(l, n, pairs, par):
                pe.wait_ge(w13_in[l][par], 32 * pairs + 32)
                pe.wait_ge(y_added[l], NT * n + 1)
                for m in range(4):
                    if m >= 2:
                        pe.wait_ge(silu_done[l], 4 * n + (m - 1))
                        pe.wait_ge(hid_done[l], 4 * n + (m - 1))
                    for w, first, done in ((W1, 4 * (m % 2), moe_g[l]), (W3, 4 * (m % 2) + 2, moe_u[l])):
                        for k in range(KC):
                            for s in range(2):
                                last = nc.tensor.matmul(bank[:, first + s, 0:NTOK // 2],
                                                        weights(w[par])[:, k, P * m:P * m + P],
                                                        xT[:, k, NTOK // 2 * s:NTOK // 2 * (s + 1)],
                                                        start=(k == 0), stop=(k == KC - 1))
                        last.then_inc(done, 1)
                pe.wait_ge(w2_in[l][par], 16 * (pairs) + 16)
                pe.wait_ge(hid_done[l], 4 * n + 4)
                for t in range(NT):
                    if t == 4:
                        pe.wait_ge(y_added[l], NT * n + 2)
                    for j in range(2):
                        for m in range(4):
                            last = nc.tensor.matmul(bank[0:ROWS[t], 2 * (t % 4) + j, :], hid[:, m, tok(t)],
                                                    weights(W2[par], 4)[:, m, 512 * j:512 * j + 512],
                                                    start=(m == 0), stop=(m == 3))
                    last.then_inc(moe_y[l], 1)

            pe.wait_ge(const_in, 16)
            for kind, *a in steps:
                if kind == "T":
                    step_T(*a)
                elif kind == "u":
                    step_u()
                elif kind == "P":
                    step_P(*a)
                elif kind == "A":
                    step_A(*a)
                elif kind == "O":
                    step_O(*a)
                elif kind == "Ub":
                    step_U(*a)
                elif kind == "y":
                    step_y(*a)
                elif kind == "R":
                    step_R(*a)
                elif kind == "router":
                    lists(*a)
                elif kind == "experts":
                    experts(*a)

        @block.scalar
        def _(act):
            chain = [0]

            def link(ins):
                chain[0] += 1
                ins.then_inc(act_step, 1)
                act.wait_ge(act_step, chain[0])

            def copy_out(key, dst, src):
                return nc.scalar.copy(dst, src)

            def read(ins):
                ins.then_inc(bank_read["act"], 1)

            def log_and_exp_table():
                nc.scalar.add_instruction(mybir.InstLoadActFuncSet(
                    name=nc.get_next_instruction_name(), engine=mybir.EngineType.Activation,
                    act_func_set_id=LN_EXP_SET))

            log_and_exp_table()

            def step_N(n, t):
                r = ROWS[t]
                if n == 0:
                    act.wait_ge(zeros_set, 1)
                    act.wait_ge(x_in[t], 16)
                elif n in (1, 3):
                    taken(act, ("y", n // 2, t, 1))
                    if t == 0:
                        act.wait_ge(bank_filled, number[("dsa" if n == 1 else "diff", "q", NT - 1)] + 1)
                else:
                    act.wait_ge(h_added, NT * (n - 2) + 2 * (t + 1))
                if NT * n + t > 0:
                    act.wait_ge(squared, NT * n + t)
                nc.scalar.activation(junk_of[n][0:r, :], h[0:r, t, :], ACT.Square,
                                     accum_out=ssq[0:r, n, t:t + 1]).then_inc(squared, 1)
                act.wait_ge(squared, NT * n + t + 1)
                link(nc.scalar.activation(logm[0:r, n, t:t + 1], ssq[0:r, n, t:t + 1], ACT.Ln,
                                          bias=const[0:r, C_EPS:C_EPS + 1], scale=1.0 / DM))
                nc.scalar.activation(root[0:r, n, t:t + 1], logm[0:r, n, t:t + 1], ACT.Exp, scale=-0.5)\
                  .then_inc(root_ready, 1)

            def step_P(mech, t, item):
                r = ROWS[t]
                own = keys_at(t)[2]
                nf = 3 if mech == "dsa" else 4
                tile = tiles_before[mech] + t
                if item == "cache":
                    for b in range(2):
                        src = filled(act, (mech, "cache", b))[:, 0:P * nf].rearrange("p (f n) -> p f n", f=nf)
                        read(nc.scalar.copy(kT[:, 0:nf, SEQ + P * b:SEQ + P * b + P], src))
                elif item == "k" and mech == "sb":
                    b = filled(act, (mech, "k", t))
                    if t > 0:
                        act.wait_ge(bank_filled, number[(mech, "kT", t - 1)] + 1)
                    act.wait_ge(out_rows, 16 * (2 * NT + t))
                    read(nc.scalar.copy(rows[0:r, 0:512], b[0:r, :]))
                elif item == "v":
                    b = filled(act, (mech, "v", t))
                    if mech == "sb":
                        act.wait_ge(out_vals, 16 * NT)
                        if t == 0:
                            act.wait_ge(h_added, 2 * 4)
                    else:
                        act.wait_ge(out_vals, 16 * (NT + (t + 1 if t < 4 else NT)))
                        act.wait_ge(out_filled, head_no("sb", 3 if t < 4 else 4, 7) + 1)
                    read(nc.scalar.copy(vodd[0:r, own_block(t), :], b[0:r, :]))
                elif item == "kT":
                    b = filled(act, (mech, "kT", t))
                    read(nc.scalar.copy(kT[:, 0:nf, own:own + r],
                                        b[:, 0:P * nf].rearrange("p (f n) -> p f n", f=nf)[:, :, 0:r]))
                elif item == "qiT":
                    b = filled(act, (mech, "qiT", t))
                    read(nc.scalar.copy(qiT[:, t % 2, :, 0:r],
                                        b[:, 0:2 * P].rearrange("p (f n) -> p f n", f=2)[:, :, 0:r]))
                elif item == "qT":
                    b = filled(act, (mech, "qT", t))
                    read(nc.scalar.copy(qT[:, tile % 2, :, 0:r],
                                        b[:, :].rearrange("p (f n) -> p f n", f=4)[:, :, 0:r]))
                elif item[0:2] == "ix":
                    nk, hd = keys_at(t)[1], int(item[2])
                    b = filled(act, (mech, item, t))
                    if 4 * t + hd > 0:
                        act.wait_ge(index_ready, 4 * t + hd)
                    read(nc.scalar.activation(idxrel[0:r, 0:nk], b[0:r, 0:nk], ACT.Relu))

            def turned(mech, t, hd):
                r, blocks, n = ROWS[t], key_blocks(t), head_no(mech, t, hd)
                b = filled(act, (mech, "pT", t, hd))
                if n >= 2:
                    act.wait_ge(out_filled, n - 1)
                if t < 4:
                    nb = len(blocks)
                    read(nc.scalar.copy(probT[:, n % 2, 0:nb, 0:r],
                                        b[:, 0:P * nb].rearrange("p (b n) -> p b n", b=nb)))
                else:
                    nc.scalar.copy(probT[:, n % 2, 0:2, 0:r],
                                   b[:, 0:2 * P].rearrange("p (b n) -> p b n", b=2)[:, :, 0:r])
                    read(nc.scalar.copy(probT[0:DEC, n % 2, 2, 0:r], b[0:DEC, 2 * P:2 * P + r]))

            def step_A(mech, g):
                count = HEADS[mech]
                if 0 <= g - LAG[mech] < NT * count:
                    turned(mech, *divmod(g - LAG[mech], count))
                if g < NT * count:
                    t, hd = divmod(g, count)
                    r, nk, n = ROWS[t], keys_at(t)[1], head_no(mech, t, hd)
                    if mech == "dsa":
                        taken(act, (mech, "s", t, hd, 0))
                        if n >= 2:
                            prob_turned(act, mech, n)
                        if hd == 0 and t >= 2:
                            act.wait_ge(out_read, t - 1)
                        nc.scalar.activation(prob_of(mech, n)[0:r, 0:nk], score[0:r, n % 2, 0:nk], ACT.Exp,
                                             bias=least[0:r, n % 16:n % 16 + 1], scale=-1.0,
                                             accum_out=rowsum[0:r, n % 16:n % 16 + 1]).then_inc(prob_ready, 1)
                    elif mech == "sb":
                        lp = logp[0:r, n % 2, 0:nk]
                        act.wait_ge(abs_ready, n - heads_before["sb"] + 1)
                        link(nc.scalar.activation(lp, lp, ACT.Exp, scale=-1.0))
                        nc.scalar.activation(lp, lp, ACT.Ln, bias=1.0).then_inc(soft_ready, 1)
                    else:
                        for c in range(2):
                            n = map_no(mech, t, hd, c)
                            taken(act, (mech, "s", t, hd, c))
                            if n - maps_before["diff"] >= 4:
                                act.wait_ge(prob_ready, head_no(mech, t, hd) - 1)
                            nc.scalar.activation(expo[0:r, n % 4, 0:nk], score[0:r, n % 2, 0:nk], ACT.Exp,
                                                 bias=least[0:r, n % 16:n % 16 + 1], scale=-1.0,
                                                 accum_out=rowsum[0:r, n % 16:n % 16 + 1])\
                              .then_inc(exp_done, 1)
                if mech == "sb" and 0 <= g - 1 < NT * count:
                    t, hd = divmod(g - 1, count)
                    n = head_no(mech, t, hd)
                    act.wait_ge(expo_in, n - heads_before["sb"] + 1)
                    pr = prob_of(mech, n)[0:ROWS[t], 0:keys_at(t)[1]]
                    nc.scalar.activation(pr, pr, ACT.Exp).then_inc(prob_ready, 1)

            def step_F(mech, t):
                if mech == "diff":
                    r = ROWS[t]
                    act.wait_ge(osq_ready, t + 1)
                    link(nc.scalar.activation(oln[0:r, :], oms[0:r, :], ACT.Ln))
                    nc.scalar.activation(ors[0:r, :], oln[0:r, :], ACT.Exp, scale=-0.5).then_inc(ors_ready, 1)

            def step_O(mech, t):
                r = ROWS[t]
                src = filled(act, (mech, "oT", t))[:, :].rearrange("p (f n) -> p f n", f=4)[:, :, 0:r]
                f = 0 if mech == "sb" else 4
                if mech == "diff":
                    if t == 0:
                        act.wait_ge(lam_exps, 2)
                    read(nc.scalar.activation(mixT[:, f:f + 4, tok(t)], src, ACT.Copy, scale=gain_out))
                else:
                    read(nc.scalar.copy(mixT[:, f:f + 4, tok(t)], src))

            def step_U(g):
                for key, lo_, hi_ in ((("dsa", "a", g), 0, SEQ), (("dsa", "as", g), SEQ, NTOK)):
                    b = filled(act, key)
                    read(nc.scalar.activation(mixT[:, g, lo_:hi_], b[:, 0:hi_ - lo_], ACT.Copy,
                                              scale=scale_pool[:, g:g + 1]))

            def router(l):
                act.wait_ge(route_in, l + 1)
                nc.scalar.activation(r_exp, r_arg, ACT.Exp).then_inc(route_exp, 1)

            def all_tokens(l):
                with act.Fori(0, NE // 2) as i:
                    for par in range(2):
                        n = 2 * i + par
                        for m in range(4):
                            act.wait_ge(moe_g[l], 4 * n + (m + 1))
                            if m >= 2:
                                act.wait_ge(hid_done[l], 4 * n + (m - 1))
                            nc.scalar.activation(silu[:, m % 2, :, :],
                                                 bank[:, 4 * (m % 2):4 * (m % 2) + 2, 0:NTOK // 2],
                                                 ACT.Silu).then_inc(silu_done[l], 1)

            def own_silu(l, e):
                act.wait_ge(up_done[l], e + 1)
                if e > 0:
                    act.wait_ge(ghid_done[l], e)
                nc.scalar.activation(gsilu, bank[:, 2 + 2 * (e % 2), 0:4 * CAP], ACT.Silu)\
                  .then_inc(gsilu_done[l], 1)

            def own_rows(l, e):
                act.wait_ge(down_done[l], e + 1)
                if e >= 2:
                    act.wait_ge(y_stored[l][e % 2], 16 * (e // 2))
                nc.scalar.copy(yrow[0:CAP, e % 2, :].rearrange("p (j n) -> p j n", j=2), bank[0:CAP, 6:8, :])\
                  .then_inc(yrow_ready[l], 1)
                act.wait_ge(yrow_ready[l], e + 1)
                act.dma_start(y_dram[l][CAP * e:CAP * e + CAP, :], yrow[0:CAP, e % 2, :])\
                   .then_inc(y_stored[l][e % 2], 16)

            def experts(l):
                full = crowded(act, l)
                with act.If(full):
                    all_tokens(l)
                with act.Else():
                    for e in range(NE):
                        own_silu(l, e)
                        if e > 0:
                            own_rows(l, e - 1)
                    own_rows(l, NE - 1)

            def step_u():
                for f in range(4):
                    b = filled(act, ("u", f))
                    read(nc.scalar.copy(uT[:, f, HIST:HIST + SEQ], b))
                b = filled(act, ("us",))
                read(nc.scalar.copy(uT[:, :, USAM:UEXT], b[:, 0:4 * DEC].rearrange("p (f n) -> p f n", f=4)))
                b = filled(act, ("hist",))
                read(nc.scalar.copy(uT[:, :, HIST + SEQ:USAM],
                                    b[:, 0:64].rearrange("p (f n) -> p f n", f=4)[:, :, 0:HIST]))
                for key, dst, row in ((("pool_p",), pool_p, poolout), (("pool_s",), pool_s, histrow)):
                    b = filled(act, key)
                    read(nc.scalar.copy(row[0:HIST, :], b[0:HIST, :]))
                    taken(act, key)
                    act.dma_start(dst[0, 0], row[0:HIST, :]).then_inc(out_pool, 16)

            def step_Z(t):
                act.wait_ge(gained, t + 1)
                act.wait_ge(scale_ready, t + 1)
                y = fin[0:ROWS[t], t, :]
                nc.scalar.activation(y, y, ACT.Copy, scale=rstd[0:ROWS[t], 4, t:t + 1]).then_inc(fin_ready, 1)

            def step_lambda():
                act.wait_ge(lam_dots, 1)
                nc.scalar.activation(lam_exp, lam_dot, ACT.Exp).then_inc(lam_exps, 1)

            act.dma_start(g_norm[:, 0, :], norm_mix[0].rearrange("(p k) -> p k", k=KC)).then_inc(gain_in, 16)
            act.wait_ge(const_in, 16)
            for kind, *a in steps:
                if kind == "N":
                    step_N(*a)
                elif kind == "u":
                    step_u()
                elif kind == "P":
                    step_P(*a)
                elif kind == "A":
                    step_A(*a)
                elif kind == "F":
                    step_F(*a)
                elif kind == "O":
                    step_O(*a)
                elif kind == "Ub":
                    if a[0] == 0:
                        act.wait_ge(small_in, 16 * SMALL_LOADS)
                    step_U(*a)
                elif kind == "router":
                    router(*a)
                elif kind == "experts":
                    experts(*a)
                    log_and_exp_table()
                elif kind == "Z":
                    step_Z(*a)
                elif kind == "lambda":
                    step_lambda()

        @block.vector
        def _(dve):
            chain = [0]
            tt = nc.vector.tensor_tensor

            def link(ins):
                chain[0] += 1
                ins.then_inc(dve_step, 1)
                dve.wait_ge(dve_step, chain[0])

            def read(ins, key):
                ins.then_inc(bank_read["dve"], 1)
                dve.wait_ge(bank_read["dve"], rank[key])

            link(nc.vector.memset(stats[:, :], 1.0))
            link(nc.vector.memset(logits, 0.0))
            nc.vector.memset(uT[:, :, 0:HIST], 0.0).then_inc(zeros_set, 1)

            def step_X(n, t):
                r = ROWS[t]
                dve.wait_ge(root_ready, NT * n + t + 1)
                y, m = root[0:r, n, t:t + 1], newton_m[0:r, :]
                link(nc.vector.tensor_scalar(m, ssq[0:r, n, t:t + 1], 1.0 / DM, EPS, ALU.mult, ALU.add))
                link(nc.vector.scalar_tensor_tensor(out=newton[0:r, :], in0=y, scalar=m, in1=y, op0=ALU.mult,
                                                    op1=ALU.mult))
                link(nc.vector.tensor_scalar(newton[0:r, :], newton[0:r, :], -0.5, 1.5, ALU.mult, ALU.add))
                last = tt(rstd[0:r, n, t:t + 1], y, newton[0:r, :], ALU.mult)
                if n == 4:
                    last.then_inc(scale_ready, 1)
                    dve.wait_ge(scale_ready, t + 1)
                    return
                link(last)
                if t >= 3:
                    dve.wait_ge(bank_filled, number[("xT", n, t - 3, 1)] + 1)
                    if n in (1, 3):
                        dve.wait_ge(x_stored[n // 2][t % 3], 16 * (t // 3))
                nc.vector.tensor_scalar(xn(n, t)[0:r, :], h[0:r, t, :], rstd[0:r, n, t:t + 1], None,
                                        ALU.mult).then_inc(xn_ready, 1)

            def step_T(n, t):
                r = ROWS[t]
                for j in range(2):
                    key = ("xT", n, t, j)
                    b = filled(dve, key)[:, :].rearrange("p (k n) -> p k n", k=4)[:, :, 0:r]
                    g = g_norm[:, n, 4 * j:4 * j + 4].unsqueeze(2).broadcast_to([P, 4, r])
                    read(tt(xT[:, 4 * j:4 * j + 4, tok(t)], b, g, ALU.mult), key)

            def rope_products(bank_ap, t, c, n, at_):
                r = ROWS[t]
                hd = n // HD
                x4 = bank_ap[0:r, c:c + n].rearrange("p (h s e) -> p h s e", s=2, e=32)
                for table, dst in ((cos, ropeA), (sin, ropeB)):
                    tab = table[0:r, t, :].unsqueeze(1).unsqueeze(1).broadcast_to([r, hd, 2, 32])
                    last = tt(dst[0:r, at_:at_ + n].rearrange("p (h s e) -> p h s e", s=2, e=32), x4, tab,
                              ALU.mult)
                return last

            def rope_free(mech, t, part):
                n = rope_no(mech, t, part)
                if n > 0:
                    dve.wait_ge(rope_out, n)

            def step_P(mech, t, item):
                r = ROWS[t]
                key = (mech, item, t)
                if item in ("kv", "ki", "k", "q") and reader.get(key) == "dve":
                    b = filled(dve, key)
                if item == "kv":
                    if t == 0:
                        dve.wait_ge(out_pool, 32)
                    rope_free(mech, t, 0)
                    rope_products(b, t, 0, 128, 0)
                    rope_products(b, t, 256, 256, 128)
                    read(nc.vector.tensor_copy(vdsa[0:r, own_block(t), :], b[0:r, 128:256]), key)
                elif item == "ki":
                    rope_products(b, t, 0, 64, 384)
                    read(nc.vector.tensor_scalar(w_idx[0:r, t % 2, :], b[0:r, 64:68], 0.0625, None,
                                                 ALU.mult), key)
                elif item[0:2] == "ix":
                    index(t, int(item[2]))
                elif item == "q" and mech == "sb":
                    if t > 0:
                        dve.wait_ge(bank_filled, number[(mech, "qT", t - 1)] + 1)
                    else:
                        dve.wait_ge(out_rows, 16 * 2 * NT)
                    read(nc.vector.tensor_copy(rows[0:r, 512:1024], b[0:r, :]), key)
                elif item == "q" or (item == "k" and mech == "diff"):
                    rope_free(mech, t, 0 if item == "k" else 1)
                    read(rope_products(b, t, 0, 512, 0), key)

            def index(t, hd):
                r, nk = ROWS[t], keys_at(t)[1]
                acc = idxacc[0:r, 0:nk]
                adm = const[0:r, C_CHUNK + 512 - nk:C_CHUNK + 512] if t < 4 else \
                    const[0:r, C_CHUNK + 128:C_CHUNK + 128 + nk]
                taken(dve, ("dsa", f"ix{hd}", t))
                nc.vector.scalar_tensor_tensor(out=acc, in0=idxrel[0:r, 0:nk],
                                               scalar=w_idx[0:r, t % 2, hd:hd + 1],
                                               in1=adm if hd == 0 else acc, op0=ALU.mult, op1=ALU.add)\
                  .then_inc(index_ready, 1)
                dve.wait_ge(index_ready, 4 * t + hd + 1)
                if t == 0 and hd == 3:
                    link(nc.vector.tensor_copy(selected[0:r, 0, 0:nk], adm))

            def select_rounds(t, lo_, hi_):
                r, nk = ROWS[t], keys_at(t)[1]
                total = (PROMPT_SEL if t < 4 else SAMPLE_SEL) // 8
                acc = idxacc[0:r, 0:nk]
                for i in range(lo_, min(hi_, total)):
                    link(nc.vector.max(top8[0:r, :], acc))
                    link(nc.vector.match_replace(acc, top8[0:r, :], acc, TAKEN))
                    if i == total - 1:
                        link(nc.vector.tensor_scalar(selected[0:r, t % 2, 0:nk], acc, 2.0 * NEG, NEG,
                                                     ALU.is_ge, ALU.mult))

            def scores_of(mech, t, hd):
                r, nk = ROWS[t], keys_at(t)[1]
                causal = {"dsa": None, "sb": C_CAUSAL, "diff": C_CHUNK}[mech]
                if causal is None:
                    mask_ = selected[0:r, t % 2, 0:nk]
                elif t < 4:
                    mask_ = const[0:r, causal + 512 - nk:causal + 512]
                else:
                    mask_ = const[0:r, causal + 128:causal + 128 + nk]
                for c in range(2 if mech == "diff" else 1):
                    key = (mech, "s", t, hd, c)
                    b = filled(dve, key)
                    n = map_no(mech, t, hd, c)
                    m = n - maps_before[mech]
                    sc = score[0:r, n % 2, 0:nk]
                    if mech == "sb":
                        if m >= 2:
                            dve.wait_ge(expo_in, m - 1)
                        read(nc.vector.scalar_tensor_tensor(out=sc, in0=b[0:r, 0:nk], scalar=0.125,
                                                            in1=mask_, op0=ALU.mult, op1=ALU.add), key)
                        if m >= 2:
                            dve.wait_ge(tail_ready, m - 1)
                        nc.vector.scalar_tensor_tensor(out=logp[0:r, n % 2, 0:nk], in0=sc, scalar=-1.0, in1=sc,
                                                       op0=ALU.mult, op1=ALU.max).then_inc(abs_ready, 1)
                        continue
                    if mech == "dsa" and m >= 2:
                        dve.wait_ge(prob_ready, n - 1)
                    if mech == "diff":
                        if m >= 2:
                            dve.wait_ge(exp_done, m - 1)
                        else:
                            dve.wait_ge(expo_in, 8 * NT)
                    read(nc.vector.tensor_tensor_reduce(sc, b[0:r, 0:nk], mask_, -0.125, 3e38, ALU.add,
                                                        ALU.min, least[0:r, n % 16:n % 16 + 1]), key)

            def step_A(mech, g):
                count = HEADS[mech]
                if g < NT * count:
                    t, hd = divmod(g, count)
                    scores_of(mech, t, hd)
                    if mech == "dsa" and t + 1 < NT:
                        select_rounds(t + 1, 2 * hd, 2 * hd + 2)
                if not 0 <= g - 1 < NT * count:
                    return
                t, hd = divmod(g - 1, count)
                r, nk, n = ROWS[t], keys_at(t)[1], head_no(mech, t, hd)
                if mech == "sb":
                    m = n - heads_before["sb"]
                    dve.wait_ge(soft_ready, m + 1)
                    lp, sc, tl = (x[0:r, n % 2, 0:nk] for x in (logp, score, tail))
                    link(nc.vector.scalar_tensor_tensor(out=lp, in0=sc, scalar=0.0, in1=lp, op0=ALU.max,
                                                        op1=ALU.add))
                    if m >= 2:
                        dve.wait_ge(expo_in, m - 1)
                    nc.vector.tensor_tensor_scan(tl[:, ::-1], lp[:, ::-1], lp[:, ::-1], 0.0, ALU.add,
                                                 ALU.bypass).then_inc(tail_ready, 1)
                elif mech == "diff":
                    m0 = map_no(mech, t, hd, 0)
                    dve.wait_ge(exp_done, m0 - maps_before["diff"] + 2)
                    c0 = m0 % 16
                    link(nc.vector.reciprocal(rinv[0:r, c0:c0 + 2], rowsum[0:r, c0:c0 + 2]))
                    link(nc.vector.tensor_scalar(rlam[0:r, :], rinv[0:r, c0 + 1:c0 + 2], lam[0:r, :], None,
                                                 ALU.mult))
                    e1 = expo[0:r, (m0 + 1) % 4, 0:nk]
                    link(nc.vector.tensor_scalar(e1, e1, rlam[0:r, :], None, ALU.mult))
                    prob_turned(dve, mech, n)
                    nc.vector.scalar_tensor_tensor(out=prob_of(mech, n)[0:r, 0:nk],
                                                   in0=expo[0:r, m0 % 4, 0:nk],
                                                   scalar=rinv[0:r, c0:c0 + 1], in1=e1, op0=ALU.mult,
                                                   op1=ALU.subtract).then_inc(prob_ready, 1)

            def step_F(mech, t):
                r = ROWS[t]
                tile = tiles_before[mech] + t
                dve.wait_ge(out_filled, head_no(mech, t, HEADS[mech] - 1) + 1)
                out = bank[0:r, NB + tile % 2, :]
                o = orow[0:r, tile % 2, :]
                if tile >= 2:
                    m2, t2 = MECHS[(tile - 2) // NT], (tile - 2) % NT
                    dve.wait_ge(bank_filled, number[(m2, "oT", t2)] + 1)
                if mech == "dsa":
                    c = 8 * (t % 2)
                    link(nc.vector.reciprocal(rinv[0:r, c:c + 8], rowsum[0:r, c:c + 8]))
                    tt(o.rearrange("p (h d) -> p h d", h=8), out.rearrange("p (h d) -> p h d", h=8),
                       rinv[0:r, c:c + 8].unsqueeze(2).broadcast_to([r, 8, HD]), ALU.mult)\
                      .then_inc(out_read, 1)
                elif mech == "sb":
                    nc.vector.tensor_copy(o, out).then_inc(out_read, 1)
                else:
                    link(nc.vector.tensor_copy(o, out))
                    for hd in range(4):
                        sl = slice(P * hd, P * hd + P)
                        ins = nc.vector.tensor_tensor_reduce(odd_junk[0:r, sl], o[:, sl], o[:, sl], 1.0, 0.0,
                                                             ALU.mult, ALU.add, osq[0:r, hd:hd + 1])
                        link(ins)
                    nc.vector.tensor_scalar(oms[0:r, :], osq[0:r, :], 1.0 / P, EPS, ALU.mult, ALU.add)\
                      .then_inc(osq_ready, 1)
                    dve.wait_ge(ors_ready, t + 1)
                    o3 = o.rearrange("p (h d) -> p h d", h=4)
                    tt(o3, o3, ors[0:r, :].unsqueeze(2).broadcast_to([r, 4, P]), ALU.mult)\
                      .then_inc(out_read, 1)

            def step_U(g):
                w = WINDOWS[g]
                dve.wait_ge(sums_ready, g + 1)
                s = (sumA, sumB)[g % 2]
                if g > 0:
                    dve.wait_ge(bank_filled, number[("dsa", "as", g - 1)] + 1)
                link(nc.vector.scalar_tensor_tensor(out=pooled, in0=s[:, HIST:HIST + SEQ],
                                                    scalar=1.0 / w, in1=uT[:, g, HIST:HIST + SEQ],
                                                    op0=ALU.mult, op1=ALU.subtract))
                link(nc.vector.scalar_tensor_tensor(out=pooled_s, in0=s[:, USAM:UEXT],
                                                    scalar=1.0 / w, in1=uT[:, g, USAM:UEXT],
                                                    op0=ALU.mult, op1=ALU.subtract))
                head = pooled[:, 0:16]
                link(tt(head, s[:, HIST:HIST + 16], const[:, C_RCNT + 16 * g:C_RCNT + 16 * g + 16], ALU.mult))
                tt(head, head, uT[:, g, HIST:HIST + 16], ALU.subtract).then_inc(pooled_ready, 1)

            def step_y(layer, t, j):
                key = ("y", layer, t, j)
                b = filled(dve, key)
                hh = h[0:ROWS[t], t, 512 * j:512 * j + 512]
                read(tt(hh, b[0:ROWS[t], :], hh, ALU.add), key)

            def step_R(l, t):
                key = ("router", l, t)
                r = ROWS[t]
                read(tt(logits[0:r, t, :], filled(dve, key)[0:r, 0:20], b_router[0:r, l, :], ALU.add), key)

            def router(l):
                dve.wait_ge(out_rows, 16 * (2 * NT if l == 0 else 4 * NT))
                dve.wait_ge(out_vals, 16 * (NT if l == 0 else 3 * NT))

                def part(a, n):
                    return route[:, a:a + n * NT].rearrange("p (t n) -> p t n", t=NT)

                js = const[:, C_IOTA:C_IOTA + 4].unsqueeze(1).broadcast_to([P, NT, 4])
                gmax, v1, v2, low = part(50, 1), part(55, 1), part(60, 1), part(65, 1)
                g_hot, hot1, hot2, eq, e_sel = (part(70 + 20 * i, 4) for i in range(5))
                e_all = part(170, 16)
                w_1, w_2, gs = part(250, 1), part(255, 1), part(260, 1)
                x_exp, g_exp = r_exp[:, 0:5].unsqueeze(2), r_exp[:, 5:25].rearrange("p (t n) -> p t n", t=NT)
                x_arg, g_arg = r_arg[:, 0:5].unsqueeze(2), r_arg[:, 5:25].rearrange("p (t n) -> p t n", t=NT)

                def bc(x, n=4):
                    return x.broadcast_to([P, NT, n])

                def first_max(src, top, hot):
                    link(nc.vector.tensor_reduce(top[:, :, 0], src, AX_X, ALU.max))
                    link(tt(eq, src, bc(top), ALU.is_equal))
                    link(nc.vector.scalar_tensor_tensor(out=eq, in0=eq, scalar=-8.0, in1=js, op0=ALU.mult,
                                                        op1=ALU.add))
                    link(nc.vector.tensor_reduce(low[:, :, 0], eq, AX_X, ALU.min))
                    link(tt(hot, eq, bc(low), ALU.is_equal))

                lg, le = logits[:, :, 0:4], logits[:, :, 4:20]
                first_max(lg, gmax, g_hot)
                link(tt(g_arg, lg, bc(gmax), ALU.subtract))
                le4 = le.rearrange("p t (g j) -> p t g j", g=4)
                ea4 = e_all.rearrange("p t (g j) -> p t g j", g=4)
                link(tt(ea4, le4, g_hot.unsqueeze(3).broadcast_to([P, NT, 4, 4]), ALU.mult))
                link(nc.vector.tensor_reduce(e_sel, ea4.rearrange("p t g j -> p t j g"), AX_X, ALU.add))
                first_max(e_sel, v1, hot1)
                link(nc.vector.scalar_tensor_tensor(out=e_sel, in0=hot1, scalar=-3e38, in1=e_sel,
                                                    op0=ALU.mult, op1=ALU.add))
                first_max(e_sel, v2, hot2)
                tt(x_arg, v2, v1, ALU.subtract).then_inc(route_in, 1)
                for c, hot in ((0, hot1), (1, hot2)):
                    link(tt(chosen[:, c].rearrange("p (t g j) -> p t g j", t=NT, g=4),
                            g_hot.unsqueeze(3).broadcast_to([P, NT, 4, 4]),
                            hot.unsqueeze(2).broadcast_to([P, NT, 4, 4]), ALU.mult))
                for c in range(2):
                    tt(token_at[:, NT * c:NT * c + NT, :], chosen[:, c].rearrange("p (t n) -> p t n", t=NT),
                       const[:, C_TOKEN:C_TOKEN + NT].unsqueeze(2).broadcast_to([P, NT, NE]), ALU.mult)
                link(nc.vector.tensor_scalar(upto, const[:, C_CAUSAL + 384:C_CAUSAL + 512], 0.5 * NEG, None,
                                             ALU.is_lt))
                link(nc.vector.memset(ones, 1.0))
                tt(mask, chosen[:, 0], chosen[:, 1], ALU.add)\
                  .then_inc(mask_ready, 1)
                dve.wait_ge(route_exp, l + 1)
                link(nc.vector.tensor_reduce(gs[:, :, 0], g_exp, AX_X, ALU.add))
                link(nc.vector.scalar_tensor_tensor(out=w_2, in0=x_exp, scalar=1.0, in1=gs, op0=ALU.add,
                                                    op1=ALU.mult))
                link(nc.vector.reciprocal(w_1, w_2))
                link(tt(w_2, w_1, x_exp, ALU.mult))
                link(tt(hot1, hot1, bc(w_1), ALU.mult))
                link(tt(hot2, hot2, bc(w_2), ALU.mult))
                link(tt(hot1, hot1, hot2, ALU.add))
                g4 = gate.rearrange("p t (g j) -> p t g j", g=4)
                tt(g4, g_hot.unsqueeze(3).broadcast_to([P, NT, 4, 4]),
                   hot1.unsqueeze(2).broadcast_to([P, NT, 4, 4]), ALU.mult).then_inc(y_added[l], 1)
                dve.wait_ge(y_added[l], 1)
                lists(l)

            def lists(l):
                key = ("rank", l)
                b = filled(dve, key)
                place3 = place.rearrange("p (t n) -> p t n", t=NT)
                spot3 = spot.rearrange("p (t n) -> p t n", t=NT)
                link(nc.vector.memset(place, 0.0))
                nc.vector.tensor_scalar(place[:, 0:4 * NE], b[:, 0:4 * NE], -1.0, None, ALU.add)
                nc.vector.tensor_scalar(place[0:DEC, 4 * NE:], b[0:DEC, 4 * NE:5 * NE], -1.0, None, ALU.add)
                read(nc.vector.tensor_reduce(most, b[:, NT * NE:NT * NE + NE], AX_X, ALU.max), key)
                link(nc.vector.tensor_copy(most_int, most))
                iota = const[:, C_IOTA:C_IOTA + CAP]
                link(nc.vector.scalar_tensor_tensor(
                    out=spot3, in0=iota[:, 0:NE].unsqueeze(1).broadcast_to([P, NT, NE]), scalar=float(CAP),
                    in1=place3, op0=ALU.mult, op1=ALU.add))
                for src, dst in ((place, place_c), (spot, spot_c)):
                    link(tt(picked, chosen, src.unsqueeze(1).broadcast_to([P, 2, NT * NE]), ALU.mult))
                    link(nc.vector.tensor_reduce(dst, picked.rearrange("p c (t n) -> p (c t) n", t=NT), AX_X,
                                                 ALU.add))
                link(tt(at_place, iota.unsqueeze(1).broadcast_to([P, 2 * NT, CAP]),
                        place_c.unsqueeze(2).broadcast_to([P, 2 * NT, CAP]), ALU.is_equal))
                nc.vector.tensor_copy(y_rows, spot_c).then_inc(lists_in, 1)
                key = ("list", l)
                b = filled(dve, key)
                read(nc.vector.tensor_copy(tokens_of[0:CAP, :], b[0:CAP, 0:NE]), key)

            def all_tokens(l):
                with dve.Fori(0, NE // 2) as i:
                    for par in range(2):
                        n = 2 * i + par
                        for m in range(4):
                            dve.wait_ge(silu_done[l], 4 * n + (m + 1))
                            dve.wait_ge(moe_u[l], 4 * n + (m + 1))
                            tt(hid[:, m, :].rearrange("p (s n) -> p s n", s=2), silu[:, m % 2, :, :],
                               bank[:, 4 * (m % 2) + 2:4 * (m % 2) + 4, 0:NTOK // 2], ALU.mult)\
                              .then_inc(hid_done[l], 1)
                        for t in range(NT):
                            r = ROWS[t]
                            dve.wait_ge(moe_y[l], NT * n + (t + 1))
                            hh = h[0:r, t, :].rearrange("p (j n) -> p j n", j=2)
                            nc.vector.scalar_tensor_tensor(
                                out=hh, in0=bank[0:r, 2 * (t % 4):2 * (t % 4) + 2, :],
                                scalar=gate[0:r, t, bass.ds(2 * i + par, 1)], in1=hh, op0=ALU.mult,
                                op1=ALU.add).then_inc(y_added[l], 1)
                        dve.wait_ge(y_added[l], NT * n + (NT + 1))

            def own_turned(l, e):
                dve.wait_ge(xg_turned[l], e + 1)
                if e >= 2:
                    dve.wait_ge(up_done[l], e - 1)
                g = g_norm[:, 2 * l + 1, :].rearrange("p (b k) -> p b k", b=2).unsqueeze(3)\
                    .broadcast_to([P, 2, 4, CAP])
                tt(xgT[:, e % 2].rearrange("p (b k) n -> p b k n", b=2),
                   bank[:, 0:2, 0:4 * CAP].rearrange("p b (k n) -> p b k n", k=4), g, ALU.mult)\
                  .then_inc(xgT_ready[l], 1)

            def own_hid(l, e):
                dve.wait_ge(gsilu_done[l], e + 1)
                if e >= 2:
                    dve.wait_ge(down_done[l], e - 1)
                tt(ghid[:, e % 2].rearrange("p m n -> p (m n)"), gsilu,
                   bank[:, 3 + 2 * (e % 2), 0:4 * CAP], ALU.mult).then_inc(ghid_done[l], 1)

            def own_tokens(l):
                own_turned(l, 0)
                for e in range(NE):
                    if e + 1 < NE:
                        own_turned(l, e + 1)
                    own_hid(l, e)

            def step_C(l, t):
                r = ROWS[t]
                dve.wait_ge(picked_in[l][t], 32)
                for c, y in ((0, first_y), (1, second_y)):
                    w = (route[:, 250:255], route[:, 255:260])[c]
                    nc.vector.scalar_tensor_tensor(out=h[0:r, t, :], in0=y[0:r, t, :], scalar=w[0:r, t:t + 1],
                                                   in1=h[0:r, t, :], op0=ALU.mult, op1=ALU.add)\
                      .then_inc(h_added, 1)
                    dve.wait_ge(h_added, 2 * NT * l + 2 * t + c + 1)

            def experts(l):
                full = crowded(dve, l)
                with dve.If(full):
                    all_tokens(l)
                with dve.Else():
                    own_tokens(l)

            def step_lambda():
                dots = lam_in.rearrange("p (a n) -> p a n", a=4)
                for i in range(2):
                    link(nc.vector.tensor_tensor_reduce(lam_tmp, dots[:, 2 * i, :], dots[:, 2 * i + 1, :], 1.0,
                                                        0.0, ALU.mult, ALU.add, lam_dot[:, i:i + 1]))
                nc.vector.tensor_scalar(gain_out, gain_diff, 1.0 - LAM_INIT, None, ALU.mult)\
                  .then_inc(lam_dots, 1)
                dve.wait_ge(lam_exps, 1)
                link(tt(lam, lam_exp[:, 0:1], lam_exp[:, 1:2], ALU.subtract))
                nc.vector.tensor_scalar(lam, lam, LAM_INIT, None, ALU.add).then_inc(lam_exps, 1)
                dve.wait_ge(lam_exps, 2)

            dve.wait_ge(const_in, 16)
            dve.wait_ge(gain_in, 16)
            for kind, *a in steps:
                if kind == "X":
                    step_X(*a)
                elif kind == "T":
                    step_T(*a)
                elif kind == "P":
                    step_P(*a)
                elif kind == "A":
                    step_A(*a)
                elif kind == "F":
                    step_F(*a)
                elif kind == "Uv":
                    step_U(*a)
                elif kind == "y":
                    step_y(*a)
                elif kind == "C":
                    step_C(*a)
                elif kind == "R":
                    if a == [0, 0]:
                        dve.wait_ge(small_in, 16 * SMALL_LOADS)
                    step_R(*a)
                elif kind == "router":
                    router(*a)
                elif kind == "experts":
                    experts(*a)
                elif kind == "lambda":
                    step_lambda()

        @block.gpsimd
        def _(pool):
            chain = [0]

            def link(ins):
                chain[0] += 1
                ins.then_inc(pool_step, 1)
                pool.wait_ge(pool_step, chain[0])

            gtt = nc.gpsimd.tensor_tensor

            def rotate(dst, src_at, n, t, dup=False):
                r = ROWS[t]
                hd = n // HD
                a, b = (x[0:r, src_at:src_at + n].rearrange("p (h s e) -> p h s e", s=2, e=32)
                        for x in (ropeA, ropeB))
                for s, op in ((0, ALU.subtract), (1, ALU.add)):
                    x, y = a[:, :, s, :], b[:, :, 1 - s, :]
                    if dup:
                        d = dst.rearrange("p (h u s e) -> p h u s e", u=2, s=2, e=32)[:, :, :, s, :]
                        x, y = (z.unsqueeze(2).broadcast_to([r, hd, 2, 32]) for z in (x, y))
                    else:
                        d = dst.rearrange("p (h s e) -> p h s e", s=2, e=32)[:, :, s, :]
                    last = gtt(d, x, y, op)
                return last

            def store(mech, t, what):
                r = ROWS[t]
                sl = slice(P * t, P * t + P) if t < 4 else slice(0, DEC)
                kd, vd = {"dsa": ((dsak_p, dsav_p), (dsak_s, dsav_s)), "sb": ((sbk_p, sbv_p), (sbk_s, sbv_s)),
                          "diff": ((dfk_p, dfv_p), (dfk_s, dfv_s))}[mech][t // 4]
                if what == "v":
                    taken(pool, (mech, "kv" if mech == "dsa" else "v", t))
                    src = (vdsa if mech == "dsa" else vodd)[0:r, own_block(t), :]
                    pool.dma_start(rows2d(vd)[sl, :], src).then_inc(out_vals, 16)
                elif mech == "dsa":
                    src = rows[0:r, 0:256].rearrange("p (g u d) -> p g u d", g=2, u=2)[:, :, 0, :]
                    pool.dma_start(kd[0, 0, sl], src).then_inc(out_rows, 16)
                    pool.dma_start((idxk_p, idxk_s)[t // 4][0, 0, sl], rows[0:r, 512:576])\
                        .then_inc(out_rows, 16)
                else:
                    kd = kd if mech == "sb" else kd.rearrange("a b s g c d -> a b s (g c) d")
                    pool.dma_start(rows2d(kd)[sl, :], rows[0:r, 0:512]).then_inc(out_rows, 16)

            def step_P(mech, t, item):
                r = ROWS[t]
                before = (mech, t - 1) if t > 0 else {"dsa": None, "sb": ("dsa", 4), "diff": ("sb", 4)}[mech]
                if item in ("ki", "k"):
                    if mech == "sb":
                        taken(pool, (mech, "k", t))
                    else:
                        if before:
                            pool.wait_ge(bank_filled, number[(before[0], "qiT" if mech == "dsa" else "kT",
                                                              before[1])] + 1)
                            pool.wait_ge(out_rows, 16 * {"dsa": 2 * t, "diff": 3 * NT + t}[mech])
                        taken(pool, (mech, item, t))
                        if mech == "dsa":
                            rotate(rows[0:r, 0:256], 0, 128, t, dup=True)
                            rotate(rows[0:r, 256:512], 128, 256, t)
                            rotate(rows[0:r, 512:640], 384, 64, t, dup=True).then_inc(rope_out, 1)
                        else:
                            rotate(rows[0:r, 0:512], 0, 512, t).then_inc(rope_out, 1)
                        pool.wait_ge(rope_out, rope_no(mech, t, 0) + 1)
                    store(mech, t, "k")
                if item in ("ki", "v"):
                    store(mech, t, "v")
                if item == "q" and mech != "sb":
                    if before:
                        pool.wait_ge(bank_filled, number[(before[0], "qT", before[1])] + 1)
                    taken(pool, (mech, "q", t))
                    q_at = 640 if mech == "dsa" else 512
                    rotate(rows[0:r, q_at:q_at + 512], 0, 512, t).then_inc(rope_out, 1)

            def step_A(mech, g):
                if mech != "sb" or not 0 <= g - 1 < 8 * NT:
                    return
                t, hd = divmod(g - 1, 8)
                r, nk, n = ROWS[t], keys_at(t)[1], head_no(mech, t, hd)
                pool.wait_ge(tail_ready, n - heads_before["sb"] + 1)
                prob_turned(pool, mech, n)
                gtt(prob_of(mech, n)[0:r, 0:nk], score[0:r, n % 2, 0:nk], tail[0:r, n % 2, 0:nk],
                    ALU.subtract).then_inc(expo_in, 1)

            def step_X(n, t):
                if n in (1, 3):
                    pool.wait_ge(xn_ready, NT * n + t + 1)
                    pool.dma_start(x_dram[n // 2][P * t:P * t + ROWS[t], :], xn(n, t)[0:ROWS[t], :])\
                        .then_inc(x_stored[n // 2][t % 3], 16)

            def sums(g):
                if g == 0:
                    taken(pool, ("hist",))
                    pool.wait_ge(zeros_set, 1)
                src, width = uT[:, g, :], 1
                if g >= 2:
                    pool.wait_ge(pooled_ready, g - 1)
                for i in range(g + 1):
                    dst = (sumA, sumB)[(g - i + g) % 2] if False else (sumA, sumB)[(g + (g - i)) % 2]
                    first = 2 * width - 1
                    if g >= 1:
                        pool.wait_ge(pooled_ready, g)
                    ins = gtt(dst[:, first:UEXT], src[:, first:UEXT], src[:, first - width:UEXT - width], ALU.add)
                    if i == g:
                        ins.then_inc(sums_ready, 1)
                    else:
                        link(ins)
                    src, width = dst, 2 * width

            def gain(t):
                r = ROWS[t]
                if t == 0:
                    pool.wait_ge(gfin_in, 16)
                pool.wait_ge(h_added, 2 * NT + 2 * (t + 1))
                gtt(fin[0:r, t, :], h[0:r, t, :], gfin[0:r, :], ALU.mult).then_inc(gained, 1)

            def own_tokens(l):
                all_x_stored(pool, l)
                for e in range(NE):
                    if e >= 3:
                        pool.wait_ge(xg_turned[l], e - 2)
                    pool.indirect_dma_start(
                        out=xg[0:CAP, e % 3, :], out_offset=None, in_=x_dram[l],
                        in_offset=bass.IndirectOffsetOnAxis(tokens_of[0:CAP, e:e + 1], 0))\
                        .then_inc(xg_in[l][e % 3], 16)
                for r in range(2):
                    pool.wait_ge(y_stored[l][r], 16 * (NE // 2))
                for t in range(NT):
                    for c, y in ((0, first_y), (1, second_y)):
                        pool.indirect_dma_start(
                            out=y[0:ROWS[t], t, :], out_offset=None, in_=y_dram[l],
                            in_offset=bass.IndirectOffsetOnAxis(y_rows[0:ROWS[t], NT * c + t:NT * c + t + 1], 0))\
                            .then_inc(picked_in[l][t], 16)

            def experts(l):
                full = crowded(pool, l)
                with pool.If(full):
                    pool.wait_ge(y_added[l], NE * NT + 1)
                    for t in range(NT):
                        for y in (first_y, second_y):
                            pool.memset(y[:, t, :], 0.0).then_inc(picked_in[l][t], 16)
                with pool.Else():
                    own_tokens(l)

            for kind, *a in steps:
                if kind == "P":
                    step_P(*a)
                elif kind == "A":
                    step_A(*a)
                elif kind == "X":
                    step_X(*a)
                elif kind == "Us":
                    sums(*a)
                elif kind == "C" and a[0] == 1:
                    gain(a[1])
                elif kind == "experts":
                    experts(*a)


SMALL_LOADS = 3 + 2 + 2 * 5 + 2 * 2 + 1

_INS = ['x_prompt', 'x_sample', 'cache_pool', 'cache_dsa_k', 'cache_dsa_v', 'cache_idx_k', 'cache_sb_k',
        'cache_sb_v', 'cache_diff_k', 'cache_diff_v', 'norm_mix', 'norm_ffn', 'norm_final', 'w_in_even',
        'w_pool', 'pool_scale', 'w_out_even', 'w_in_odd', 'diff_lambda', 'diff_subln', 'w_out_odd',
        'moe_w_group', 'moe_b_group', 'moe_w_expert', 'moe_b_expert', 'moe_w1', 'moe_w3', 'moe_w2']
_OUTS = [(1, 512, 1024), (1, 32, 1024),
         (1, 1, 15, 512), (1, 1, 512, 2, 64), (1, 1, 512, 2, 64), (1, 1, 512, 64),
         (1, 1, 512, 8, 64), (1, 1, 512, 8, 64), (1, 1, 512, 4, 2, 64), (1, 1, 512, 4, 128),
         (1, 1, 15, 512), (1, 1, 32, 2, 64), (1, 1, 32, 2, 64), (1, 1, 32, 64),
         (1, 1, 32, 8, 64), (1, 1, 32, 8, 64), (1, 1, 32, 4, 2, 64), (1, 1, 32, 4, 128)]


def _constants():
    import numpy as np
    c = np.zeros((P, C_N), np.float32)
    half = HD // 2
    inv = (np.float32(10000.0) ** (-np.arange(half, dtype=np.float32) / np.float32(half))).astype(np.float32)
    p = np.arange(P)
    for t in range(NT):
        pos = (P * t if t < 4 else PAST) + p
        ang = pos.astype(np.float32)[:, None] * inv[None, :]
        c[:, C_COS + 32 * t:C_COS + 32 * t + 32] = np.cos(ang)
        c[:, C_SIN + 32 * t:C_SIN + 32 * t + 32] = np.sin(ang)
    c[:, C_ID:C_ID + P] = np.eye(P)
    k = np.arange(P)
    c[:, C_CHUNK + 384:C_CHUNK + 512] = np.where(k[None, :] < (p[:, None] // CHUNK + 1) * CHUNK, 0.0, NEG)
    c[:, C_CAUSAL + 384:C_CAUSAL + 512] = np.where(k[None, :] < p[:, None], 0.0, NEG)
    for g, w in enumerate(WINDOWS):
        c[:, C_RCNT + 16 * g:C_RCNT + 16 * g + 16] = 1.0 / np.minimum(np.arange(16) + 1, w)
    c[:, C_IOTA:C_IOTA + CAP] = np.arange(CAP)
    c[:, C_EPS] = EPS
    c[:, C_TOKEN:C_TOKEN + NT] = P * np.arange(NT)[None, :] + p[:, None]
    return c


def kernel(**inputs):
    import numpy as _np
    import concourse.bacc as _bacc
    from concourse import mybir as _mybir
    from concourse.bass_utils import run_bass_kernel_spmd as _run

    nc = _bacc.Bacc("TRN2", target_bir_lowering=False, num_devices=1)
    arrays, args = {}, []
    for name in _INS:
        arrays[f"in_{name}"] = _np.ascontiguousarray(inputs[name])
    arrays["in_constants"] = _constants()
    for name, a in arrays.items():
        args.append(nc.dram_tensor(name, a.shape, _mybir.dt.from_np(a.dtype), kind="ExternalInput").ap())
    for i, shape in enumerate(_OUTS):
        args.append(nc.dram_tensor(f"out_{i}", shape, _mybir.dt.float32, kind="ExternalOutput").ap())
    stream_kernel(nc, *args)
    r = _run(nc, [arrays], core_ids=[0])
    return tuple(r.results[0][f"out_{i}"] for i in range(len(_OUTS)))
```
